# Optimizing a Trainium2 kernel written in Bass

```python
import jax, jax.numpy as jnp
from jax import lax
import numpy as np
import math

D_MODEL = 1024
BATCH = 1
SEQ = 512
DEPTH = 1

PLE_DIM = 256
MLA_HEADS = 4
QK_NOPE_DIM = 128
QK_ROPE_DIM = 64
QK_HEAD_DIM = QK_NOPE_DIM + QK_ROPE_DIM
V_HEAD_DIM = 128
Q_LORA_RANK = 256
KV_LORA_RANK = 128
ROPE_THETA = 10000.0
MLA_WIDTH = MLA_HEADS * V_HEAD_DIM
Q_BLOCK = 128
MLSTM_HEADS = 4
MLSTM_HEAD_DIM = 128
MLSTM_WIDTH = MLSTM_HEADS * MLSTM_HEAD_DIM
CONV_WIDTH = 4
CHUNK = 64
D_MIX = MLA_WIDTH + MLSTM_WIDTH
IN_SIZES = (Q_LORA_RANK, KV_LORA_RANK, QK_ROPE_DIM, MLSTM_WIDTH, MLSTM_WIDTH, MLSTM_WIDTH, MLSTM_WIDTH, MLSTM_HEADS, MLSTM_HEADS)
D_IN = sum(IN_SIZES)
D_FF = ((8 * D_MODEL + 3 * 256 - 1) // (3 * 256)) * 256
EPS = 1e-6


def rms_norm(x, g):
    xf = x.astype(jnp.float32)
    y = xf * lax.rsqrt(jnp.mean(xf * xf, axis=-1, keepdims=True) + EPS)
    return (y * g.astype(jnp.float32)).astype(x.dtype)

def split_cols(z, sizes):
    offs = np.cumsum(sizes)[:-1].tolist()
    return jnp.split(z, offs, axis=-1)

def rope_cos_sin(positions):
    inv_freq = ROPE_THETA ** (-jnp.arange(0, QK_ROPE_DIM, 2, dtype=jnp.float32) / QK_ROPE_DIM)
    ang = positions.astype(jnp.float32)[..., None] * inv_freq
    return jnp.cos(ang), jnp.sin(ang)

def apply_rope(t, cos, sin):
    tf = t.astype(jnp.float32)
    t1, t2 = tf[..., :QK_ROPE_DIM // 2], tf[..., QK_ROPE_DIM // 2:]
    return jnp.concatenate([t1 * cos - t2 * sin, t2 * cos + t1 * sin], axis=-1).astype(t.dtype)

def causal_mla(q, k, v):
    B, S, H, _ = q.shape
    nb = S // Q_BLOCK
    qb = (q * (QK_HEAD_DIM ** -0.5)).reshape(B, nb, Q_BLOCK, H, QK_HEAD_DIM).transpose(1, 0, 3, 2, 4)
    key_pos = jnp.arange(S)

    def one_block(args):
        q_blk, blk = args
        s = jnp.einsum('bhqd,bkhd->bhqk', q_blk, k).astype(jnp.float32)
        q_pos = blk * Q_BLOCK + jnp.arange(Q_BLOCK)
        s = jnp.where(key_pos[None, :] <= q_pos[:, None], s, -jnp.inf)
        pr = jax.nn.softmax(s, axis=-1).astype(v.dtype)
        return jnp.einsum('bhqk,bkhv->bqhv', pr, v)

    out = lax.map(one_block, (qb, jnp.arange(nb)))
    return out.transpose(1, 0, 2, 3, 4).reshape(B, S, H * V_HEAD_DIM)

def causal_dwconv(t, w, b):
    S = t.shape[1]
    tp = jnp.pad(t, ((0, 0), (CONV_WIDTH - 1, 0), (0, 0)))
    acc = b
    for j in range(CONV_WIDTH):
        acc = acc + w[j] * tp[:, j:j + S]
    return acc

def mlstm_chunkwise(q, k, v, i_pre, f_pre):
    out_dtype = q.dtype
    B, S, NH, DH = q.shape
    nc = S // CHUNK
    f32 = jnp.float32

    def chunks4(t):
        return t.astype(f32).reshape(B, nc, CHUNK, NH, DH).transpose(1, 0, 3, 2, 4)

    def chunks3(t):
        return t.astype(f32).reshape(B, nc, CHUNK, NH).transpose(1, 0, 3, 2)

    qc_all = chunks4(q)
    kc_all = chunks4(k) * (DH ** -0.5)
    vc_all = chunks4(v)
    ic_all = chunks3(i_pre)
    fc_all = jax.nn.log_sigmoid(chunks3(f_pre))
    tril = jnp.tril(jnp.ones((CHUNK, CHUNK), dtype=bool))

    def step(carry, xs):
        C, n, m = carry
        qc, kc, vc, ic, fc = xs
        b = jnp.cumsum(fc, axis=-1)
        g = b[..., -1]
        d = b[..., :, None] - b[..., None, :] + ic[..., None, :]
        d = jnp.where(tril, d, -jnp.inf)
        m_inter = b + m[..., None]
        m_j = jnp.maximum(m_inter, d.max(axis=-1))
        s = jnp.einsum('bhld,bhsd->bhls', qc, kc) * jnp.exp(d - m_j[..., None])
        inter = jnp.exp(m_inter - m_j)
        num = jnp.einsum('bhls,bhsv->bhlv', s, vc) + inter[..., None] * jnp.einsum('bhld,bhdv->bhlv', qc, C)
        den = s.sum(axis=-1) + inter * jnp.einsum('bhld,bhd->bhl', qc, n)
        h = num / jnp.maximum(jnp.abs(den), jnp.exp(-m_j))[..., None]
        a = g[..., None] - b + ic
        m_new = jnp.maximum(g + m, a.max(axis=-1))
        decay = jnp.exp(g + m - m_new)
        w = jnp.exp(a - m_new[..., None])
        C_new = decay[..., None, None] * C + jnp.einsum('bhs,bhsd,bhsv->bhdv', w, kc, vc)
        n_new = decay[..., None] * n + jnp.einsum('bhs,bhsd->bhd', w, kc)
        return (C_new, n_new, m_new), h

    init = (jnp.zeros((B, NH, DH, DH), f32), jnp.zeros((B, NH, DH), f32), jnp.zeros((B, NH), f32))
    _, h = lax.scan(step, init, (qc_all, kc_all, vc_all, ic_all, fc_all))
    return h.transpose(1, 0, 3, 2, 4).reshape(B, S, NH, DH).astype(out_dtype)

def first_inputs(seed: int = 0) -> dict:
    key = jax.random.key(seed)
    ks = jax.random.split(key, 26)
    f32 = jnp.float32

    def nrm(k, shape, scale):
        return jax.random.normal(k, shape, f32) * scale

    def gain(k, shape):
        return 1.0 + 0.05 * jax.random.normal(k, shape, f32)

    L = DEPTH
    x = nrm(ks[0], (BATCH, SEQ, D_MODEL), 1.0)
    p = nrm(ks[1], (DEPTH, BATCH, SEQ, PLE_DIM), 1.0)
    offset = jax.random.randint(ks[2], (BATCH, 1), 0, 1024, dtype=jnp.int32)
    positions = (offset + jnp.arange(SEQ, dtype=jnp.int32)[None, :]).astype(jnp.int32)
    return {
        "x": x,
        "p": p,
        "positions": positions,
        "attn_pre_norm": gain(ks[3], (L, D_MODEL)),
        "attn_post_norm": gain(ks[4], (L, D_MODEL)),
        "w_in": nrm(ks[5], (L, D_MODEL, D_IN), D_MODEL ** -0.5),
        "q_norm": gain(ks[6], (L, Q_LORA_RANK)),
        "kv_norm": gain(ks[7], (L, KV_LORA_RANK)),
        "w_uq": nrm(ks[8], (L, Q_LORA_RANK, MLA_HEADS * QK_HEAD_DIM), Q_LORA_RANK ** -0.5),
        "w_ukv": nrm(ks[9], (L, KV_LORA_RANK, MLA_HEADS * (QK_NOPE_DIM + V_HEAD_DIM)), KV_LORA_RANK ** -0.5),
        "conv_w": nrm(ks[10], (L, CONV_WIDTH, 2 * MLSTM_WIDTH), CONV_WIDTH ** -0.5),
        "conv_b": nrm(ks[11], (L, 2 * MLSTM_WIDTH), 0.02),
        "gate_bias_i": nrm(ks[12], (L, MLSTM_HEADS), 0.1),
        "gate_bias_f": 3.0 + nrm(ks[13], (L, MLSTM_HEADS), 0.5),
        "mlstm_norm": gain(ks[14], (L, MLSTM_WIDTH)),
        "w_out": nrm(ks[15], (L, D_MIX, D_MODEL), D_MIX ** -0.5),
        "ffn_pre_norm": gain(ks[16], (L, D_MODEL)),
        "ffn_post_norm": gain(ks[17], (L, D_MODEL)),
        "w_gate": nrm(ks[18], (L, D_MODEL, D_FF), D_MODEL ** -0.5),
        "w_up": nrm(ks[19], (L, D_MODEL, D_FF), D_MODEL ** -0.5),
        "w_down": nrm(ks[20], (L, D_FF, D_MODEL), D_FF ** -0.5),
        "w_ple_proj": nrm(ks[21], (L, PLE_DIM, D_MODEL), PLE_DIM ** -0.5),
        "w_ple_gate": nrm(ks[22], (L, D_MODEL, D_MODEL), D_MODEL ** -0.5),
    }

def first_block(x, p, positions, attn_pre_norm, attn_post_norm, w_in, q_norm, kv_norm, w_uq, w_ukv,
              conv_w, conv_b, gate_bias_i, gate_bias_f, mlstm_norm, w_out, ffn_pre_norm, ffn_post_norm,
              w_gate, w_up, w_down, w_ple_proj, w_ple_gate):
    B, S, _ = x.shape
    cos, sin = rope_cos_sin(positions)
    hd = (B, S, MLSTM_HEADS, MLSTM_HEAD_DIM)
    h = x
    for i in range(DEPTH):
        u = rms_norm(h, attn_pre_norm[i])
        c_q, c_kv, k_rope, m_q, m_k, m_v, m_o, m_i, m_f = split_cols(u @ w_in[i], IN_SIZES)

        q = (rms_norm(c_q, q_norm[i]) @ w_uq[i]).reshape(B, S, MLA_HEADS, QK_HEAD_DIM)
        kv = (rms_norm(c_kv, kv_norm[i]) @ w_ukv[i]).reshape(B, S, MLA_HEADS, QK_NOPE_DIM + V_HEAD_DIM)
        q_nope, q_pe = q[..., :QK_NOPE_DIM], q[..., QK_NOPE_DIM:]
        k_nope, v = kv[..., :QK_NOPE_DIM], kv[..., QK_NOPE_DIM:]
        q_pe = apply_rope(q_pe, cos[:, :, None], sin[:, :, None])
        k_pe = apply_rope(k_rope, cos, sin)[:, :, None]
        q = jnp.concatenate([q_nope, q_pe], axis=-1)
        k = jnp.concatenate([k_nope, jnp.broadcast_to(k_pe, (B, S, MLA_HEADS, QK_ROPE_DIM))], axis=-1)
        mla_out = causal_mla(q, k, v)

        qk = jax.nn.silu(causal_dwconv(jnp.concatenate([m_q, m_k], axis=-1), conv_w[i], conv_b[i]))
        mq, mk = qk[..., :MLSTM_WIDTH], qk[..., MLSTM_WIDTH:]
        hm = mlstm_chunkwise(mq.reshape(hd), mk.reshape(hd), m_v.reshape(hd),
                             m_i + gate_bias_i[i], m_f + gate_bias_f[i])
        hm = rms_norm(hm, mlstm_norm[i].reshape(MLSTM_HEADS, MLSTM_HEAD_DIM)).reshape(B, S, MLSTM_WIDTH)
        mlstm_out = jax.nn.sigmoid(m_o) * hm

        mix = jnp.concatenate([mla_out, mlstm_out], axis=-1) @ w_out[i]
        h = h + rms_norm(mix, attn_post_norm[i])

        f = rms_norm(h, ffn_pre_norm[i])
        f = (jax.nn.silu(f @ w_gate[i]) * (f @ w_up[i])) @ w_down[i]
        h = h + rms_norm(f, ffn_post_norm[i])

        h = h + jax.nn.sigmoid(h @ w_ple_gate[i]) * (p[i] @ w_ple_proj[i])
    return h


DEPTH_2 = 2

N_MIXERS = 2
N_META = 16
N_HEADS = 8
HEAD_DIM = D_MODEL // (2 * N_HEADS)
V_DIM = 2 * HEAD_DIM
CONV_WIDTH_2 = 3
CONV_GROUPS = 8
D_FF_2 = 4 * D_MODEL
RMS_EPS = 1e-6
N_ATTN_LAYERS = (DEPTH_2 + 1) // 2
N_CONV_LAYERS = DEPTH_2 // 2


def _rmsnorm(x, g):
    xf = x.astype(jnp.float32)
    y = xf * lax.rsqrt(jnp.mean(xf * xf, axis=-1, keepdims=True) + RMS_EPS)
    return (y * g.astype(jnp.float32)).astype(x.dtype)

def _alibi_slopes(n_heads):
    return jnp.exp2(-8.0 * jnp.arange(1, n_heads + 1, dtype=jnp.float32) / n_heads)

def _lambda_init(layer_idx):
    return 0.8 - 0.6 * math.exp(-0.3 * layer_idx)

def _query_blocks(total_len):
    blocks = [(0, N_META)]
    start = N_META
    while start < total_len:
        end = min(start + Q_BLOCK, total_len)
        blocks.append((start, end))
        start = end
    return blocks

def _diff_attention(h, w_in, w_out, lam_vec, subln_g, lam_init):
    bsz, L, _ = h.shape
    qkv = jnp.einsum('bld,de->ble', h, w_in)
    q, k, v = jnp.split(qkv, 3, axis=-1)
    q = q.reshape(bsz, L, N_HEADS, 2, HEAD_DIM)
    k = k.reshape(bsz, L, N_HEADS, 2, HEAD_DIM)
    v = v.reshape(bsz, L, N_HEADS, V_DIM)
    lv = lam_vec.astype(jnp.float32)
    lam = jnp.exp(jnp.sum(lv[0] * lv[1])) - jnp.exp(jnp.sum(lv[2] * lv[3])) + lam_init
    slopes = _alibi_slopes(N_HEADS)
    scale = HEAD_DIM ** -0.5
    pos = jnp.arange(L, dtype=jnp.int32)
    outs = []
    for qs, qe in _query_blocks(L):
        s = jnp.einsum('bqhcd,bkhcd->bhcqk', q[:, qs:qe], k[:, :qe]).astype(jnp.float32) * scale
        dist = (pos[qs:qe, None] - pos[None, :qe]).astype(jnp.float32)
        bias = -slopes[:, None, None, None] * dist
        s = jnp.where(dist >= 0, s + bias, -jnp.inf)
        p = jax.nn.softmax(s, axis=-1)
        a = (p[:, :, 0] - lam * p[:, :, 1]).astype(v.dtype)
        outs.append(jnp.einsum('bhqk,bkhe->bqhe', a, v[:, :qe]))
    o = jnp.concatenate(outs, axis=1)
    o = _rmsnorm(o, subln_g) * (1.0 - lam_init)
    return jnp.einsum('ble,ed->bld', o.reshape(bsz, L, N_HEADS * V_DIM), w_out)

def _short_conv(h, w_in, conv_w, w_out):
    bcu = jnp.einsum('bld,de->ble', h, w_in)
    b_gate, c_gate, u = jnp.split(bcu, 3, axis=-1)
    u = c_gate * u
    y = lax.conv_general_dilated(
        u, conv_w[:, None, :].astype(u.dtype), window_strides=(1,),
        padding=[(CONV_WIDTH_2 - 1, 0)], dimension_numbers=('NWC', 'WIO', 'NWC'),
        feature_group_count=D_MODEL)
    return jnp.einsum('bld,de->ble', b_gate * y, w_out)

def _sqrelu_mlp(h, w_up, w_down):
    a = jax.nn.relu(jnp.einsum('bld,df->blf', h, w_up))
    return jnp.einsum('blf,fd->bld', a * a, w_down)

def second_inputs(seed: int = 0) -> dict:
    key = jax.random.key(seed)
    ks = jax.random.split(key, 10)
    x = jax.random.normal(ks[0], (BATCH, SEQ, D_MODEL), jnp.float32)
    meta_tokens = jax.random.normal(ks[1], (N_META, D_MODEL), jnp.float32)
    norm_g = 1.0 + 0.05 * jax.random.normal(ks[2], (DEPTH_2, 4, D_MODEL), jnp.float32)
    w_in = jax.random.normal(ks[3], (DEPTH_2, D_MODEL, 3 * D_MODEL), jnp.float32) * D_MODEL ** -0.5
    w_out = jax.random.normal(ks[4], (DEPTH_2, D_MODEL, D_MODEL), jnp.float32) * D_MODEL ** -0.5
    lambda_params = 0.1 * jax.random.normal(ks[5], (N_ATTN_LAYERS, 4, HEAD_DIM), jnp.float32)
    subln_g = 1.0 + 0.05 * jax.random.normal(ks[6], (N_ATTN_LAYERS, V_DIM), jnp.float32)
    conv_w = jax.random.normal(ks[7], (N_CONV_LAYERS, CONV_WIDTH_2, D_MODEL), jnp.float32) * CONV_WIDTH_2 ** -0.5
    w_up = jax.random.normal(ks[8], (DEPTH_2, D_MODEL, D_FF_2), jnp.float32) * D_MODEL ** -0.5
    w_down = jax.random.normal(ks[9], (DEPTH_2, D_FF_2, D_MODEL), jnp.float32) * D_FF_2 ** -0.5
    return {'x': x, 'meta_tokens': meta_tokens, 'norm_g': norm_g, 'w_in': w_in, 'w_out': w_out,
            'lambda_params': lambda_params, 'subln_g': subln_g, 'conv_w': conv_w,
            'w_up': w_up, 'w_down': w_down}

def second_block(x, meta_tokens, norm_g, w_in, w_out, lambda_params, subln_g, conv_w, w_up, w_down):
    bsz = x.shape[0]
    meta = jnp.broadcast_to(meta_tokens[None].astype(x.dtype), (bsz, N_META, D_MODEL))
    hres = jnp.concatenate([meta, x], axis=1)
    for i in range(DEPTH_2):
        h = _rmsnorm(hres, norm_g[i, 0])
        if i % N_MIXERS == 0:
            m = _diff_attention(h, w_in[i], w_out[i], lambda_params[i // N_MIXERS],
                                subln_g[i // N_MIXERS], _lambda_init(i))
        else:
            m = _short_conv(h, w_in[i], conv_w[i // N_MIXERS], w_out[i])
        hres = hres + _rmsnorm(m, norm_g[i, 1])
        h = _rmsnorm(hres, norm_g[i, 2])
        hres = hres + _rmsnorm(_sqrelu_mlp(h, w_up[i], w_down[i]), norm_g[i, 3])
    return hres[:, N_META:]


def setup_inputs(seed=0):
    out = dict(first_inputs(seed))
    for name, value in second_inputs(seed + 1).items():
        if name != "x":
            out[name + "_2"] = value
    return out


def reference(
    x, p, positions, attn_pre_norm, attn_post_norm, w_in, q_norm, kv_norm, w_uq, w_ukv, conv_w,
    conv_b, gate_bias_i, gate_bias_f, mlstm_norm, w_out, ffn_pre_norm, ffn_post_norm, w_gate,
    w_up, w_down, w_ple_proj, w_ple_gate, meta_tokens_2, norm_g_2, w_in_2, w_out_2,
    lambda_params_2, subln_g_2, conv_w_2, w_up_2, w_down_2,
):
    x = first_block(
        x, p, positions, attn_pre_norm, attn_post_norm, w_in, q_norm, kv_norm, w_uq, w_ukv,
        conv_w, conv_b, gate_bias_i, gate_bias_f, mlstm_norm, w_out, ffn_pre_norm,
        ffn_post_norm, w_gate, w_up, w_down, w_ple_proj, w_ple_gate,
    )
    return second_block(
        x, meta_tokens_2, norm_g_2, w_in_2, w_out_2, lambda_params_2, subln_g_2, conv_w_2,
        w_up_2, w_down_2,
    )


_drawn_inputs = setup_inputs


def setup_inputs(seed=0):
    import zlib

    import numpy as np

    out = dict(_drawn_inputs(seed))
    spreads = {}
    factors = {'q_norm': 4.174, 'conv_b': 3.267, 'gate_bias_i': 200.0, 'lambda_params_2': 4.699}
    for name, (base, spread) in spreads.items():
        noise = np.random.default_rng([zlib.crc32(name.encode()), seed]).standard_normal(out[name].shape)
        drawn = base * np.exp(spread * noise) if base else spread * noise
        out[name] = __import__('jax').numpy.asarray(drawn.astype(out[name].dtype))
    for name, factor in factors.items():
        out[name] = (out[name] * factor).astype(out[name].dtype)
    return out
```

```python
import math

import numpy as np

import concourse.bass as bass
from concourse import mybir
from contextlib import ExitStack

P = 128
D = 1024
KD = D // P
S = 512
META = 16
T = S + META
HALF = T // 2
BLK = 2 * KD * P
QKD = 192
FF1 = 2816 // P
CHUNKS1 = [8, 8, 6]
FF2 = 4096 // P
NCH2 = FF2 // KD
DIFF_HEADS = 8
GROUPS = 4
LAM_INIT = 0.8 - 0.6 * math.exp(-0.3 * 0)
EPS = 1e-6
NEG = -1e30

B_IN, B_UQ, B_UKV, B_OUT1, B_MLP1 = 0, 11, 12, 13, 17
B_PLEP = B_MLP1 + FF1 + 4 * len(CHUNKS1)
B_PLEG = B_PLEP + 1
B_QKV = B_PLEG + 4
B_OUT2 = B_QKV + 3 * GROUPS
B_MLP2 = B_OUT2 + 4
B_CONV = B_MLP2 + 8 * NCH2
B_OUT3 = B_CONV + 12
B_MLP3 = B_OUT3 + 4
NBLK = B_MLP3 + 8 * NCH2
MANY = {B_UQ: 4, B_UKV: 4, B_PLEP: 4}


def pair_of(block):
    return block + sum(n - 1 for b, n in MANY.items() if b < block)


SMALL = {}
NSMALL = 0
for _name, _n in [("attn_pre", 8), ("attn_post", 8), ("ffn_pre", 8), ("ffn_post", 8), ("norm2", 64),
                  ("q_norm", 2), ("kv_norm", 1), ("conv_b", 8), ("conv_w", 32), ("conv2_w", 24),
                  ("mlstm_norm", 4), ("subln", 1), ("gate_i", 1), ("gate_f", 1),
                  ("freq", 1), ("sfreq", 1)]:
    SMALL[_name] = NSMALL
    NSMALL += _n

KB_N = [S - P * kb for kb in range(4)]
KB_AT = [sum(KB_N[:kb]) for kb in range(4)]
PACK = sum(KB_N)


def build(nc, wstream, xT, metaT, pT, pos, small, lam, out):
    f32, f32r, i32 = mybir.dt.float32, mybir.dt.float32r, mybir.dt.int32
    ALU, ACT = mybir.AluOpType, mybir.ActivationFunctionType
    ctx = ExitStack()
    with ctx:
        def sb(name, shape, dt=f32):
            return ctx.enter_context(nc.sbuf_tensor(name, shape, dt))

        def sem(name):
            return ctx.enter_context(nc.semaphore(name))

        w_raw = sb("w_raw", [P, 2, BLK])
        w_hi = sb("w_hi", [P, 2, BLK], f32r)
        w_lo = sb("w_lo", [P, 2, BLK], f32r)
        h = sb("h", [P, KD, T])
        z_hi = sb("z_hi", [P, KD, T], f32r)
        z_lo = sb("z_lo", [P, KD, T], f32r)
        ARENA = 3072 + 2048 + 12288 + 4 * S
        arena = sb("arena", [P, ARENA], f32r)
        acc = sb("acc", [P, KD * T])
        tmp = sb("tmp", [P, 6 * T])
        sq = sb("sq", [P, 2, T])
        ssum = sb("ssum", [P, T])
        rr = sb("rr", [P, 2, T])
        rope_cs = sb("rope_cs", [P, 2, S])
        dist = sb("dist", [P, T])
        tri = sb("tri", [P, P])
        ident = sb("ident", [P, P])
        ones = sb("ones", [P, P])
        ones_r = sb("ones_r", [P, P], f32r)
        sm = sb("sm", [P, NSMALL])
        cols = sb("cols", [P, 120])
        eps = sb("eps", [P, 4])

        ps = ctx.enter_context(nc.psum_tensor("ps", [P, 8, 512], f32))

        def smc(name, k=0, n=1, rows=P):
            return sm[0:rows, SMALL[name] + k:SMALL[name] + k + n]

        def tt(k, n=T, rows=P):
            return tmp[0:rows, k * T:k * T + n]

        def ac(k, n=T):
            return acc[:, k * T:k * T + n]

        def a_c(part, k):
            return arena[:, part * 1536 + k * S:part * 1536 + k * S + S]

        def a_kpe(part, odd, r0=0, r1=P):
            at = 3072 + (part * 2 + odd) * S
            return arena[r0:r1, at:at + S]

        A_U = 5120

        def a_mqk(part, j):
            at = A_U + (part * 8 + j) * S
            return arena[:, at:at + S]

        def a_v(part, hh):
            at = A_U + 8192 + (part * 4 + hh) * S
            return arena[:, at:at + S]

        def a_p(part, at=0, n=PACK):
            z = (z_hi if part == 0 else z_lo)[:, :, :].rearrange("p a b -> p (a b)")
            return z[:, at:at + n]

        def a_q(part, j):
            at = A_U + (part * 6 + j) * S
            return arena[:, at:at + S]

        def a_k(part, hh):
            j = part * 4 + hh
            at = A_U + 6144 + j * S if j < 4 else A_U + 12288 + (j - 4) * S
            return arena[:, at:at + S]

        def a_pt(part, slot, n=S):
            at = (part * 2 + slot) * S
            return arena[:, at:at + n]

        def a_out(part, k, c0=0, c1=T):
            at = (part * KD + k) * T
            return arena[:, at + c0:at + c1]
        A_2 = 2 * KD * T

        def a_qk(part, which, hh):
            at = A_2 + ((part * 2 + which) * 2 + hh) * T
            return arena[:, at:at + T]

        def a_dv(part, hh, t, rows=P, nt=1):
            at = A_2 + 8 * T + ((part * 2 + hh) * 5 + t) * P
            return arena[0:rows, at:at + nt * P]

        def a_dpt(part, slot, t, rows=P, nt=1):
            at = A_2 + 8 * T + 20 * P + ((part * 2 + slot) * 5 + t) * P
            return arena[0:rows, at:at + nt * P]

        def a_hid(part, k):
            at = (part * KD + k) * T
            return arena[:, at:at + T]

        def so(hh):
            return acc[:, hh * S:hh * S + S]
        AX = [acc[:, 2048:2560], acc[:, 2560:3072]]
        G0, G1 = acc[:, 3072:3584], acc[:, 3584:4096]

        raw_in = [sem("raw_in0"), sem("raw_in1")]
        whi, wlo = sem("whi"), sem("wlo")
        ps_full, ps_free = sem("ps_full"), sem("ps_free")
        h_in = [sem(f"h_in{k}") for k in range(KD)]
        small_in, pos_in, meta_in, p_in = sem("small_in"), sem("pos_in"), sem("meta_in"), sem("p_in")
        lam_in = sem("lam_in")
        out_sem = sem("out_sem")
        zhi, zlo = sem("zhi"), sem("zlo")
        squared, summed, stat, rooted, rstd = sem("squared"), sem("summed"), sem("stat"), sem("rooted"), sem("rstd")
        scaled, resid = sem("scaled"), sem("resid")
        acc_zero = sem("acc_zero")
        consts = sem("consts")
        names = {}

        def s(name):
            if name not in names:
                names[name] = sem(name)
            return names[name]

        def wait(eng, semaphore, n):
            eng.wait_ge(semaphore, n)

        def banks(slot, o, ntok, rows=P):
            b = 4 * slot + 2 * o
            return ps[0:rows, b, 0:ntok] if ntok <= 512 else ps[0:rows, b:b + 2, 0:HALF]

        def like(ap, ntok):
            return ap if ntok <= 512 else ap.rearrange("p (a b) -> p a b", a=2)

        block = ctx.enter_context(nc.Block())

        @block.sync
        def _(sp):
            sp.dma_start(h[:, 0, META:T], xT[0]).then_inc(h_in[0], 16)
            sp.dma_start(sm[:, :], small).then_inc(small_in, 16)
            for k in range(1, KD):
                sp.dma_start(h[:, k, META:T], xT[k]).then_inc(h_in[k], 16)
            for i in range(2):
                sp.dma_start(w_raw[:, i, :], wstream[i]).then_inc(raw_in[i], 16)
            sp.dma_start(so(1).bitcast(i32), pos).then_inc(pos_in, 16)
            sp.dma_start(h[:, :, 0:META], metaT).then_inc(meta_in, 16)
            sp.dma_start(acc[:, 0:256], lam).then_inc(lam_in, 16)
            with sp.Fori(1, B_PLEP // 2 + 1) as i:
                for j in range(2):
                    sp.wait_ge(wlo, 2 * i + (j - 1))
                    sp.dma_start(w_raw[:, j, :], wstream[2 * i + j]).then_inc(raw_in[j], 16)
            sp.wait_ge(resid, 16)
            sp.dma_start(tmp[:, 0:2 * S], pT).then_inc(p_in, 16)
            with sp.Fori(B_PLEP // 2 + 1, NBLK // 2) as i:
                for j in range(2):
                    sp.wait_ge(wlo, 2 * i + (j - 1))
                    sp.dma_start(w_raw[:, j, :], wstream[2 * i + j]).then_inc(raw_in[j], 16)
            for k in range(KD):
                sp.wait_ge(resid, 8 * 5 + k + 1)
                sp.dma_start(out[k], h[:, k, META:T]).then_inc(out_sem, 16)
            sp.wait_ge(out_sem, 16 * KD)

        def act_hi(act, slot, n_raw, n_full):
            act.wait_ge(raw_in[slot], 16 * n_raw)
            if n_full is not None:
                act.wait_ge(ps_full, n_full)
            act.activation(w_hi[:, slot, :], w_raw[:, slot, :], ACT.Copy).then_inc(whi, 1)

        def used(i):
            return 2 * pair_of(i + 1)

        def act_next(act, i):
            act_hi(act, i % 2, i // 2 + 1, used(i - 2) if i >= 2 else None)

        def dve_lo(dve, i, slot):
            dve.wait_ge(whi, i + 1)
            dve.tensor_tensor(w_lo[:, slot, :], w_raw[:, slot, :], w_hi[:, slot, :].bitcast(f32),
                              ALU.subtract).then_inc(wlo, 1)

        def project(pe, wslot, slot, first_tile, nk, z, ntok, before, z_ready=None):
            if before is not None:
                pe.wait_ge(ps_free, before)
            cuts = [(0, ntok)] if ntok <= 512 else [(0, HALF), (HALF, T)]
            for k in range(nk):
                if z_ready is not None:
                    z_ready(k)
                for o in range(2):
                    at = ((first_tile + o) * nk + k) * P
                    wh, wl = w_hi[:, wslot, at:at + P], w_lo[:, wslot, at:at + P]
                    for c, (a, b) in enumerate(cuts):
                        dst = ps[:, 4 * slot + 2 * o + c, 0:b - a]
                        zh, zl = z(0, k)[:, a:b], z(1, k)[:, a:b]
                        pe.matmul(dst, wh, zh, start=(k == 0), stop=False)
                        pe.matmul(dst, wh, zl, start=False, stop=False)
                        last = pe.matmul(dst, wl, zh, start=False, stop=(k == nk - 1))
                    if k == nk - 1:
                        last.then_inc(ps_full, 1)

        def z_part(part, k):
            return (z_hi if part == 0 else z_lo)[:, k, :]

        def pe_stat(pe, si, slot, ntok, c0):
            pe.wait_ge(summed, 8 * (si + 1))
            if ntok <= 512:
                pe.matmul(ps[:, 4 * slot, 0:ntok], ones[:, :], ssum[:, c0:c0 + ntok], start=True, stop=True).then_inc(stat, 1)
            else:
                for c in range(2):
                    last = pe.matmul(ps[:, 4 * slot + c, 0:HALF], ones[:, :], ssum[:, c * HALF:(c + 1) * HALF], start=True, stop=True)
                last.then_inc(stat, 1)

        def act_root(act, si, slot, ntok, c0):
            act.wait_ge(stat, si + 1)
            dst = rr[:, si % 2, c0:c0 + ntok]
            act.activation(like(dst, ntok), banks(slot, 0, ntok), ACT.Sqrt, bias=eps[:, 0:1], scale=1.0 / D).then_inc(rooted, 1)

        def dve_rstd(dve, si, ntok, c0):
            dve.wait_ge(rooted, si + 1)
            dst = rr[:, si % 2, c0:c0 + ntok]
            dve.reciprocal(dst, dst).then_inc(rstd, 1)

        def act_square(act, si, k, src, ntok, c0):
            if 8 * si + k >= 2:
                act.wait_ge(summed, 8 * si + k - 1)
            act.activation(sq[:, k % 2, c0:c0 + ntok], src, ACT.Square).then_inc(squared, 1)

        def pool_sum(pool, si, ntok, c0):
            for k in range(KD):
                pool.wait_ge(squared, 8 * si + k + 1)
                if k == 0:
                    if si:
                        pool.wait_ge(stat, si)
                    pool.tensor_copy(ssum[:, c0:c0 + ntok], sq[:, 0, c0:c0 + ntok]).then_inc(summed, 1)
                else:
                    pool.wait_ge(summed, 8 * si + k)
                    pool.tensor_tensor(ssum[:, c0:c0 + ntok], ssum[:, c0:c0 + ntok], sq[:, k % 2, c0:c0 + ntok],
                                       ALU.add).then_inc(summed, 1)

        GAIN = {0: ("attn_pre", 0), 1: ("ffn_pre", 0), 3: ("norm2", 0), 4: ("norm2", 16), 5: ("norm2", 32), 6: ("norm2", 48)}

        def act_zhi(act, zi, k, c0):
            g = 1.0 if zi == 2 else smc(GAIN[zi][0], GAIN[zi][1] + k)
            act.activation(z_hi[:, k, 0:T - c0], h[:, k, c0:T], ACT.Copy, scale=g).then_inc(zhi, 1)

        def dve_zlo(dve, zi, k, c0):
            dve.wait_ge(zhi, 8 * zi + k + 1)
            hk, zk = h[:, k, c0:T], z_hi[:, k, 0:T - c0].bitcast(f32)
            if zi == 2:
                dve.tensor_tensor(z_lo[:, k, 0:T - c0], hk, zk, ALU.subtract).then_inc(zlo, 1)
            else:
                dve.scalar_tensor_tensor(z_lo[:, k, 0:T - c0], hk, smc(GAIN[zi][0], GAIN[zi][1] + k), zk,
                                         op0=ALU.mult, op1=ALU.subtract).then_inc(zlo, 1)

        POST = {0: ("attn_post", 0), 1: ("ffn_post", 0), 2: ("norm2", 8), 3: ("norm2", 24), 4: ("norm2", 40), 5: ("norm2", 56)}
        NEXT_Z = {0: 1, 1: 2, 2: 4, 3: 5, 4: 6}

        def act_post(act, pi, p_out, ntok, c0, nxt_c0=None):
            si = 2 * pi + 1
            for k in range(KD):
                act.wait_ge(ps_free, 2 * p_out + k + 1)
                act_square(act, si, k, ac(k)[:, c0:T], ntok, c0)
            act_root(act, si, 0, ntok, c0)
            if pi == 5:
                return
            zi = NEXT_Z[pi]
            for k in range(KD):
                act.wait_ge(resid, 8 * pi + k + 1)
                if k == 0:
                    act.wait_ge(ps_full, 2 * p_out + 8)
                act_zhi(act, zi, k, nxt_c0)
                if zi != 2:
                    act_square(act, si + 1, k, h[:, k, c0:T], ntok, c0)

        def dve_post(dve, pi, ntok, c0, nxt_c0=None):
            si = 2 * pi + 1
            dve_rstd(dve, si, ntok, c0)
            dve.wait_ge(rstd, si + 1)
            for k in range(KD + 1):
                if k < KD:
                    t = ac(k)[:, c0:T]
                    dve.scalar_tensor_tensor(t, t, smc(POST[pi][0], POST[pi][1] + k), rr[:, si % 2, c0:T],
                                             op0=ALU.mult, op1=ALU.mult).then_inc(scaled, 1)
                    dve.wait_ge(scaled, 8 * pi + k + 1)
                    dve.tensor_tensor(h[:, k, c0:T], h[:, k, c0:T], t, ALU.add).then_inc(resid, 1)
                if k and pi != 5:
                    dve_zlo(dve, NEXT_Z[pi], k - 1, nxt_c0)

        def z_ready_for(pe, zi):
            return lambda k: pe.wait_ge(zlo, 8 * zi + k + 1)


        def dve_take(dve, p, o, ntok, dst, r=None, then=None):
            dve.wait_ge(ps_full, 2 * p + o + 1)
            src = banks(p % 2, o, ntok)
            if r is None:
                dve.tensor_copy(like(dst, ntok), src).then_inc(ps_free, 1)
            else:
                dve.tensor_tensor(like(dst, ntok), src, like(r, ntok), ALU.mult).then_inc(ps_free, 1)

        def once(dve, name, n, ins):
            ins.then_inc(s(name), 1)
            dve.wait_ge(s(name), n)

        P_IN, P_UQ, P_UKV, P_OUT1, P_MLP1, P_PLEP, P_PLEG, P_QKV, P_OUT2, P_MLP2, P_CONV, P_OUT3, P_MLP3 = (
            pair_of(b) for b in (B_IN, B_UQ, B_UKV, B_OUT1, B_MLP1, B_PLEP, B_PLEG, B_QKV, B_OUT2, B_MLP2,
                                 B_CONV, B_OUT3, B_MLP3))
        RX = rr[:, 0, META:T]
        SC1 = QKD ** -0.5
        SC2 = (D // (2 * DIFF_HEADS)) ** -0.5
        SCM = P ** -0.5
        UG = 10

        def unit(u, c):
            b = u % 5
            nq, nk = (META, META) if b == 0 else (P, META + P * b)
            return nq, nk, tt((u % 2) * 2 + c, nk, nq)

        def d_parts(u):
            return 2 * (u + 1) - (u // 5 + 1)

        @block.gpsimd
        def _(pool):
            pool.memset(ident[:, :], 0.0).then_inc(consts, 1)
            pool.memset(tri[:, :], 0.0).then_inc(consts, 1)
            pool.memset(dist[:, :], 0.0).then_inc(consts, 1)
            pool.memset(eps[:, 0:1], EPS).then_inc(consts, 1)
            pool.memset(eps[:, 1:2], 1.0).then_inc(consts, 1)
            pool.memset(eps[:, 2:3], EPS / (1 - LAM_INIT) ** 2).then_inc(consts, 1)
            pool.memset(eps[:, 3:4], 0.0).then_inc(consts, 1)
            pool.memset(ones[:, :], 1.0).then_inc(consts, 1)
            pool.memset(ones_r[:, :].bitcast(f32), 1.0).then_inc(consts, 1)
            for part in range(2):
                pool.wait_ge(consts, 9 + 2 * part)
                pool.memset(a_kpe(part, 0, 64, P).bitcast(f32), 0.0).then_inc(consts, 1)
                pool.wait_ge(consts, 10 + 2 * part)
                pool.memset(a_kpe(part, 1, 0, 64).bitcast(f32), 0.0).then_inc(consts, 1)
            pool.wait_ge(consts, 13)
            pool.affine_select(out=ident[:, :], in_=ident[:, :], compare_op=ALU.not_equal, fill=1.0, base=0,
                               pattern=[[-1, P]], channel_multiplier=1).then_inc(consts, 1)
            pool.affine_select(out=tri[:, :], in_=tri[:, :], compare_op=ALU.is_ge, fill=NEG, base=0,
                               pattern=[[1, P]], channel_multiplier=-1).then_inc(consts, 1)
            pool.affine_select(out=dist[:, 0:S], in_=dist[:, 0:S], compare_op=ALU.is_ge, fill=NEG, base=S - P,
                               pattern=[[-1, S]], channel_multiplier=1).then_inc(consts, 1)
            pool_sum(pool, 0, S, META)
            pool.wait_ge(stat, 1)
            sel = ssum[0:4, 0:S].rearrange("p (a b) -> p a b", a=4)
            pool.memset(ssum[0:4, 0:S], 0.0).then_inc(s("sel"), 1)
            pool.wait_ge(s("sel"), 1)
            pool.affine_select(out=sel, in_=sel, compare_op=ALU.not_equal, fill=1.0, base=0,
                               pattern=[[-1, 4], [0, P]], channel_multiplier=1).then_inc(s("sel"), 1)
            pool.wait_ge(s("bc"), 4)
            pool_sum(pool, 1, S, META)
            pool_sum(pool, 2, S, META)

            def zero_acc(pi):
                pool.wait_ge(resid, 8 * pi + 8)
                pool.memset(acc[:, :], 0.0).then_inc(acc_zero, 1)
            zero_acc(0)
            pool_sum(pool, 3, S, META)
            pool.wait_ge(s("a_max"), 16)
            pool.iota(dist[:, :], pattern=[[1, T]], base=-(S - P + META), channel_multiplier=-1,
                      allow_small_or_imprecise_dtypes=True).then_inc(s("dist"), 1)
            pool.wait_ge(s("dist"), 1)
            pool.affine_select(out=dist[:, :], in_=dist[:, :], compare_op=ALU.is_ge, fill=NEG, base=S - P + META,
                               pattern=[[-1, T]], channel_multiplier=1).then_inc(s("dist"), 1)
            pool_sum(pool, 4, T, 0)
            pool_sum(pool, 5, T, 0)
            pool_sum(pool, 6, T, 0)
            zero_acc(2)
            pool_sum(pool, 7, T, 0)
            pool_sum(pool, 8, T, 0)
            pool_sum(pool, 9, S, META)
            pool_sum(pool, 10, S, META)
            zero_acc(4)
            pool_sum(pool, 11, S, META)

        @block.scalar
        def _(act):
            act.wait_ge(small_in, 16)
            act.wait_ge(consts, 13)
            for k in range(KD):
                act.wait_ge(h_in[k], 16)
                act_zhi(act, 0, k, META)
                act_square(act, 0, k, h[:, k, META:T], S, META)
                if k == 1:
                    act_next(act, 0)
            act_next(act, 1)
            act_root(act, 0, 1, S, META)
            act_next(act, 2)
            act.wait_ge(ps_free, 3)
            for k in range(3):
                act.activation(tt(3 + k, S), tt(k, S), ACT.Square).then_inc(s("c_sq"), 1)
            act_next(act, 3)
            act.wait_ge(s("c_stat"), 2)
            act.activation(tt(3, S), ps[:, 3, :], ACT.Sqrt, bias=eps[:, 0:1], scale=1.0 / 256).then_inc(s("c_root"), 1)
            act.activation(tt(5, S), ps[:, 7, :], ACT.Sqrt, bias=eps[:, 0:1], scale=1.0 / 128).then_inc(s("c_root"), 1)
            for k in range(3):
                act.wait_ge(s("c_norm"), k + 1)
                act.activation(a_c(0, k), tt(k, S), ACT.Copy).then_inc(s("c_hi"), 1)
            act.wait_ge(s("angle"), 2)
            act.activation(rope_cs[:, 0, :], rope_cs[:, 0, :], ACT.Sin).then_inc(s("cs"), 1)
            act.activation(rope_cs[:, 1, :], rope_cs[:, 1, :], ACT.Sin).then_inc(s("cs"), 1)
            act.wait_ge(s("lamsum"), 2)
            act.activation(cols[:, 82:84], cols[:, 80:82], ACT.Exp).then_inc(s("lamexp"), 1)
            act.wait_ge(s("kr_sum"), 1)
            act.activation(a_kpe(0, 0, 0, 64), AX[0][0:64, :], ACT.Copy).then_inc(s("kr_hi"), 1)
            act.activation(a_kpe(0, 1, 64, P), AX[0][64:P, :], ACT.Copy).then_inc(s("kr_hi"), 1)
            act.wait_ge(s("g_abs"), 1)
            act.activation(AX[0][0:4, :], AX[0][0:4, :], ACT.Exp, scale=-1.0).then_inc(s("g_exp"), 1)
            act.wait_ge(s("g_exp"), 1)
            act.activation(AX[0][0:4, :], AX[0][0:4, :], ACT.Ln, bias=eps[0:4, 1:2]).then_inc(s("g_exp"), 1)
            for j in range(8):
                if j % 2 == 0:
                    act_next(act, 4 + j // 2)
                q = j % 2
                act.wait_ge(ps_free, 2 * 3 + j + 1)
                act.activation(tt(2 + q, S), tt(q)[:, 4:4 + S], ACT.Identity, bias=smc("conv_b", j),
                               scale=smc("conv_w", 24 + j)).then_inc(s("cv_y"), 1)
                act.wait_ge(s("cv_acc"), 3 * j + 3)
                if j >= 2:
                    act.wait_ge(s("cv_lo"), j - 1)
                act.activation(tt(4 + q, S), tt(2 + q, S), ACT.Silu).then_inc(s("cv_s"), 1)
                act.wait_ge(s("cv_s"), j + 1)
                act.activation(a_mqk(0, j), tt(4 + q, S), ACT.Copy).then_inc(s("cv_hi"), 1)

            def v_hi(g):
                act.wait_ge(s("v_tr"), g + 1)
                act.activation(a_v(0, g % 4), ps[:, 3 + 4 * (g % 2), :], ACT.Copy).then_inc(s("v_hi"), 1)
            act_next(act, 8)
            act_next(act, 9)
            v_hi(0)
            v_hi(1)
            act_next(act, 10)
            for hh in range(4):
                if hh == 2:
                    v_hi(2)
                    v_hi(3)
                    act_next(act, 11)
                act.wait_ge(ps_free, 2 * 9 + hh + 1)
                act.activation(so(hh), tt(4 + hh % 2, S), ACT.Sigmoid).then_inc(s("so"), 1)
            act_next(act, 12)
            for hh in range(4):
                act.wait_ge(s("bc"), hh + 1)
                act.wait_ge(s("m_d"), 4 * hh + 4)
                act.activation(sq[:, 0, 0:S], ps[:, 5, :], ACT.Exp).then_inc(s("m_e"), 1)
                for kb in range(4):
                    e = tmp[:, KB_AT[kb]:KB_AT[kb] + KB_N[kb]]
                    gc = cols[:, 64 + 4 * kb + hh:65 + 4 * kb + hh]
                    act.activation(e[:, 0:P], tmp[:, 2560 + kb * P:2560 + kb * P + P], ACT.Exp, bias=gc).then_inc(s("m_e"), 1)
                    if kb < 3:
                        act.activation(e[:, P:], ps[:, 1, (kb + 1) * P:S], ACT.Exp, bias=gc).then_inc(s("m_e"), 1)
                act.wait_ge(s("m_p"), 4 * hh + 4)
                act.activation(a_p(0), tmp[:, PACK:2 * PACK], ACT.Copy).then_inc(s("m_hi"), 1)
                act.wait_ge(s("m_nd"), hh + 1)
                act.activation(sq[:, 1, 0:S], ps[:, 7, :], ACT.Abs).then_inc(s("m_abs"), 1)
                act.wait_ge(s("m_h"), 6 * hh + 3)
                act.activation(rr[:, 1, 0:S], rr[:, 0, 0:S], ACT.Square).then_inc(s("m_sq"), 1)
                act.wait_ge(s("m_st"), hh + 1)
                act.activation(rr[:, 1, 0:S], ps[:, 3, :], ACT.Sqrt, bias=eps[:, 0:1], scale=1.0 / P).then_inc(s("m_root"), 1)
                act.wait_ge(s("m_h"), 6 * hh + 6)
                act.activation(z_hi[:, 4 + hh, 0:S], rr[:, 0, 0:S], ACT.Copy).then_inc(s("m_zhi"), 1)
            for j in range(4):
                act.wait_ge(ps_full, 2 * P_UQ + j + 1)
                act.activation(a_q(0, j), banks((P_UQ + j // 2) % 2, j % 2, S), ACT.Copy).then_inc(s("q_hi"), 1)
            for j in range(2):
                act.wait_ge(s("qr_sum"), j + 1)
                act.activation(a_q(0, 4 + j), AX[j], ACT.Copy).then_inc(s("q_hi"), 1)
            act_next(act, 13)
            for j in range(4):
                act.wait_ge(ps_full, 2 * P_UKV + j + 1)
                act.activation(a_k(0, j), banks((P_UKV + j // 2) % 2, j % 2, S), ACT.Copy).then_inc(s("q_hi"), 1)
            for g in range(4, 8):
                v_hi(g)
            act_next(act, 14)

            def mla_exp(u):
                q = u % 2
                n = P * (u % 4 + 1)
                act.wait_ge(s("a_nmx"), u + 1)
                act.activation(tt(q, n), tt(q, n), ACT.Exp, bias=cols[:, 16 + u:17 + u], scale=SC1,
                               accum_out=cols[:, 32 + u:33 + u]).then_inc(s("a_exp"), 1)

            def mla_hi(u):
                act.wait_ge(s("a_tr"), u + 1)
                n = P * (u % 4 + 1)
                act.activation(a_pt(0, u % 2, n), ps[:, 2 + 4 * (u % 2), 0:n], ACT.Copy).then_inc(s("a_hi"), 1)

            def mla_out(u):
                act.wait_ge(s("a_pv"), u + 1)
                hh, b = divmod(u, 4)
                act.activation(z_hi[:, hh, P * b:P * b + P], ps[:, 1 + 4 * (u % 2), 0:P], ACT.Copy).then_inc(s("a_zhi"), 1)
            mla_exp(0)
            for u in range(16 + 2):
                if u + 1 < 16:
                    mla_exp(u + 1)
                if 1 <= u < 17:
                    mla_hi(u - 1)
                if u >= 2:
                    mla_out(u - 2)
            for j in range(2, 4):
                act_next(act, B_OUT1 + j)
            act_next(act, B_MLP1)
            act_post(act, 0, P_OUT1, S, META, nxt_c0=META)
            done = 0
            for c, nt in enumerate(CHUNKS1):
                b0, p0 = B_MLP1 + done + 4 * c, P_MLP1 + done + 4 * c
                for j in range(nt):
                    act_next(act, b0 + j + 1)
                    n = done + j
                    if n == 0:
                        act_root(act, 2, (P_MLP1 + 1) % 2, S, META)
                    q = n % 2
                    act.wait_ge(ps_free, 2 * (p0 + j) + 1)
                    act.activation(tt(2 + q, S), tt(q, S), ACT.Silu).then_inc(s("sw_silu"), 1)
                    act.wait_ge(s("sw_hm"), n + 1)
                    act.wait_ge(ps_full, 2 * p0)
                    act.activation(a_hid(0, j)[:, 0:S], tt(4 + q, S), ACT.Copy).then_inc(s("sw_hi"), 1)
                for j in range(4):
                    act_next(act, b0 + nt + j + 1)
                done += nt
            p_out1 = P_PLEP - 4
            act_post(act, 1, p_out1, S, META, nxt_c0=META)
            act.wait_ge(p_in, 16)
            for k in range(2):
                act.activation(a_c(0, k), tmp[:, k * S:k * S + S], ACT.Copy).then_inc(s("p_hi"), 1)
            act_next(act, B_PLEG)
            for k in range(KD):
                if k % 2 == 0:
                    act_next(act, B_PLEG + k // 2 + 1)
                act.wait_ge(ps_full, 2 * P_PLEG + k + 1)
                if k >= 2:
                    act.wait_ge(ps_free, 2 * P_PLEG + k - 1)
                act.activation(tt(2 + k % 2, S), banks((P_PLEG + k // 2) % 2, k % 2, S), ACT.Sigmoid).then_inc(s("ple_s"), 1)
            act.wait_ge(meta_in, 16)
            for k in range(KD):
                act.wait_ge(s("ple_h"), k + 1)
                act_zhi(act, 3, k, 0)
                act_square(act, 4, k, h[:, k, :], T, 0)

            def d_exp(u):
                for c in range(2):
                    act.wait_ge(s("d_nmx"), 2 * u + c + 1)
                    nq, nk, t = unit(u, c)
                    w = (u % 2) * 2 + c
                    act.activation(t, t, ACT.Exp, bias=cols[0:nq, 94 + w:95 + w], scale=SC2,
                                   accum_out=cols[0:nq, 98 + w:99 + w]).then_inc(s("d_exp"), 1)

            def d_hi(u):
                nq, nk, _ = unit(u, 0)
                act.wait_ge(s("d_tr"), u + 1)
                act.activation(a_dpt(0, u % 2, 0, META)[:, 0:nq], ps[0:META, 6 + u % 2, 0:nq], ACT.Copy).then_inc(s("d_hi"), 1)
                if nk > META:
                    act.activation(a_dpt(0, u % 2, 1, P, (nk - META) // P), ps[:, 4 + u % 2, 0:nk - META], ACT.Copy).then_inc(s("d_hi"), 1)

            for g in range(GROUPS):
                b0, p0 = B_QKV + 3 * g, P_QKV + 3 * g
                for i in range(2):
                    act_next(act, b0 + i + 1)
                    if g == 0 and i == 0:
                        act_root(act, 4, (P_QKV + 1) % 2, T, 0)
                    for o in range(2):
                        act.wait_ge(ps_free, 2 * (p0 + i) + o + 1)
                        act.activation(a_qk(0, o, i), tt(2 * i + o), ACT.Copy).then_inc(s("dq_hi"), 1)
                act_next(act, b0 + 3)
                for i in range(2):
                    act.wait_ge(s("dv_tr"), 2 * g + i + 1)
                    act.activation(a_dv(0, i, 1, P, 4), ps[:, 4 + i, :], ACT.Copy).then_inc(s("dv_hi"), 1)
                    act.activation(a_dv(0, i, 0, META), ps[0:META, 6 + i, 0:P], ACT.Copy).then_inc(s("dv_hi"), 1)
                first = UG * g
                d_exp(first)
                for u in range(first, first + UG + 1):
                    if u + 1 < first + UG:
                        d_exp(u + 1)
                    if u >= first + 1:
                        d_hi(u - 1)
                for i in range(2):
                    act.wait_ge(s("d_o"), UG * g + 5 * i + 5)
                    act.activation(sq[:, i, :], ac(2 * g + i), ACT.Square).then_inc(s("d_sq"), 1)
                    act.wait_ge(s("d_st"), 2 * g + i + 1)
                    act.activation(like(rr[:, 1, :], T), ps[:, 2 * i:2 * i + 2, 0:HALF], ACT.Sqrt, bias=eps[:, 2:3],
                                   scale=1.0 / (P * (1 - LAM_INIT) ** 2)).then_inc(s("d_root"), 1)
                    act.wait_ge(s("d_n"), 4 * g + 2 * i + 2)
                    act.activation(a_out(0, 2 * g + i), ac(2 * g + i), ACT.Copy).then_inc(s("d_ohi"), 1)
            for j in range(1, 4):
                act_next(act, B_OUT2 + j)
            act_next(act, B_MLP2)
            act_post(act, 2, P_OUT2, T, 0, nxt_c0=0)

            def act_mlp(l, b0, p0, si, ntok):
                def chunk(c, last=False):
                    head = isinstance(c, int) and c == 0
                    for j in range(KD // 2):
                        act_hi(act, (b0 + j + 1) % 2, (b0 + j + 1) // 2 + 1 + 4 * c, 2 * (p0 + j) + 16 * c)
                        if head and j == 0:
                            act_root(act, si, (p0 + 1) % 2, ntok, T - ntok)
                        for o in range(2):
                            n = FF2 * l + 2 * j + o + 8 * c
                            act.wait_ge(ps_free, 2 * (p0 + j) + o + 1 + 16 * c)
                            if not (head and n < 2):
                                act.wait_ge(s("hid_lo"), n - 1)
                            act.activation(tt(2 + o, ntok), tt(o, ntok), ACT.Square).then_inc(s("hid_a"), 1)
                        for o in range(2):
                            n = FF2 * l + 2 * j + o + 8 * c
                            act.wait_ge(s("hid_a"), n + 1)
                            act.activation(a_hid(0, 2 * j + o)[:, 0:ntok], tt(2 + o, ntok), ACT.Copy).then_inc(s("hid_hi"), 1)
                    for j in range(4, 8):
                        if not (last and j == 7):
                            act_hi(act, (b0 + j + 1) % 2, (b0 + j + 1) // 2 + 1 + 4 * c, 2 * (p0 + j) + 16 * c)
                return chunk
            mlp = act_mlp(0, B_MLP2, P_MLP2, 6, T)
            mlp(0)
            with act.Fori(1, NCH2) as c:
                mlp(c)
            act_post(act, 3, P_CONV - 4, T, 0, nxt_c0=0)
            for m in range(4):
                p0 = P_CONV + 3 * m
                for i in range(2):
                    act_next(act, B_CONV + 3 * m + i + 1)
                    if m == 0 and i == 0:
                        act_root(act, 8, (P_CONV + 1) % 2, T, 0)
                    j = 2 * m + i
                    act.wait_ge(s("sc_v"), j + 1)
                    act.activation(tt(4 + i, S), tt(2 + i)[:, META:T], ACT.Copy, scale=smc("conv2_w", 16 + j)).then_inc(s("sc_y"), 1)
                act_next(act, B_CONV + 3 * m + 3)
                for i in range(2):
                    j = 2 * m + i
                    act.wait_ge(s("sc_o"), j + 1)
                    act.activation(a_out(0, j, 0, S), tt(i, S), ACT.Copy).then_inc(s("sc_hi"), 1)
            for j in range(1, 4):
                act_next(act, B_OUT3 + j)
            act_next(act, B_MLP3)
            act_post(act, 4, P_OUT3, S, META, nxt_c0=META)
            mlp = act_mlp(1, B_MLP3, P_MLP3, 10, S)
            mlp(0)
            with act.Fori(1, NCH2 - 1) as c:
                mlp(c)
            mlp(NCH2 - 1, last=True)
            act_post(act, 5, P_MLP3 + 8 * NCH2 - 4, S, META)

        @block.vector
        def _(dve):
            dve.wait_ge(small_in, 16)
            dve.wait_ge(consts, 16)
            for k in range(KD):
                dve_zlo(dve, 0, k, META)
                if k == 1:
                    dve_lo(dve, 0, 0)
            dve_lo(dve, 1, 1)
            dve_rstd(dve, 0, S, META)
            dve.wait_ge(rstd, 1)
            for o in range(2):
                dve_take(dve, 0, o, S, tt(o, S), RX)
            dve_lo(dve, 2, 0)
            dve_take(dve, 1, 0, S, tt(2, S), RX)
            dve.wait_ge(ps_full, 4)
            dve.tensor_tensor(G0[0:4, :], ps[0:4, 6, :], RX[0:4, :], ALU.mult).then_inc(s("gate"), 1)
            dve.tensor_tensor(G1[32:36, :], ps[32:36, 6, :], RX[32:36, :], ALU.mult).then_inc(ps_free, 1)
            dve.wait_ge(pos_in, 16)
            n_ang = 0

            def ang(ins):
                nonlocal n_ang
                n_ang += 1
                once(dve, "ang", n_ang, ins)
            MAGIC = 1.5 * 2.0 ** 23
            C1 = 6.28125
            C2 = float(np.float32(np.floor((2 * math.pi - C1) * 2.0 ** 21) / 2.0 ** 21))
            C3 = 2 * math.pi - C1 - C2
            PI32 = 3.1415925
            ang(dve.tensor_copy(so(2), so(1).bitcast(i32)))
            for w, (name, off) in enumerate([("freq", 0.25), ("sfreq", 0.0)]):
                r = rope_cs[:, w, :]
                ang(dve.tensor_scalar(r, so(2), smc(name), None, ALU.mult))
                ang(dve.tensor_scalar(so(3), r, 1 / (2 * math.pi), off, ALU.mult, ALU.add))
                ang(dve.tensor_scalar(so(3), so(3), MAGIC, None, ALU.add))
                ang(dve.tensor_scalar(so(3), so(3), MAGIC, None, ALU.subtract))
                for cc in (C1, C2, C3):
                    ang(dve.scalar_tensor_tensor(r, so(3), -cc, r, op0=ALU.mult, op1=ALU.add))
                ang(dve.tensor_scalar(r, r, 2 * math.pi * off, PI32, ALU.add, ALU.min))
                dve.tensor_scalar(r, r, -PI32, None, ALU.max).then_inc(s("angle"), 1)
            dve.wait_ge(lam_in, 16)
            for w in range(2):
                dve.tensor_tensor_reduce(out=so(3)[:, 64 * w:64 * w + 64], in0=acc[:, 128 * w:128 * w + 64],
                                         in1=acc[:, 128 * w + 64:128 * w + 128], scale=1.0, scalar=0.0,
                                         op0=ALU.mult, op1=ALU.add, accum_out=cols[:, 80 + w:81 + w]).then_inc(s("lamsum"), 1)
            dve_lo(dve, 3, 1)
            for o in range(2):
                dve_take(dve, 2, o, S, AX[o], RX)
            dve.wait_ge(s("c_root"), 2)
            once(dve, "c_rcp", 1, dve.reciprocal(tt(3, S), tt(3, S)))
            once(dve, "c_rcp", 2, dve.reciprocal(tt(5, S), tt(5, S)))
            for k in range(3):
                g = smc("q_norm", k) if k < 2 else smc("kv_norm")
                dve.scalar_tensor_tensor(tt(k, S), tt(k, S), g, tt(3 if k < 2 else 5, S), op0=ALU.mult,
                                         op1=ALU.mult).then_inc(s("c_norm"), 1)
            for k in range(3):
                dve.wait_ge(s("c_hi"), k + 1)
                dve.tensor_tensor(a_c(1, k), tt(k, S), a_c(0, k).bitcast(f32), ALU.subtract).then_inc(s("c_lo"), 1)
            dve.wait_ge(s("cs"), 2)
            dve.wait_ge(ps_free, 6)
            once(dve, "kr", 1, dve.tensor_tensor(AX[0], AX[0], rope_cs[:, 0, :], ALU.mult))
            once(dve, "kr", 2, dve.tensor_tensor(AX[1], AX[1], rope_cs[:, 1, :], ALU.mult))
            dve.tensor_tensor(AX[0], AX[0], AX[1], ALU.add).then_inc(s("kr_sum"), 1)
            dve.wait_ge(s("kr_hi"), 2)
            dve.wait_ge(s("kr_sum"), 1)
            for odd, (r0, r1) in enumerate([(0, 64), (64, P)]):
                dve.tensor_tensor(a_kpe(1, odd, r0, r1), AX[0][r0:r1, :], a_kpe(0, odd, r0, r1).bitcast(f32),
                                  ALU.subtract).then_inc(s("kr_lo"), 1)
            dve.wait_ge(s("kr_lo"), 2)
            dve.wait_ge(s("lamexp"), 1)
            dve.tensor_scalar(cols[:, 84:85], cols[:, 83:84], cols[:, 82:83], LAM_INIT, ALU.subtract,
                              ALU.subtract).then_inc(s("lam"), 1)
            g0, g1, x0, x1 = G0[0:4, :], G1[0:4, :], AX[0][0:4, :], AX[1][0:4, :]
            once(dve, "g", 1, dve.tensor_copy(g1, G1[32:36, :]))
            once(dve, "g", 2, dve.tensor_scalar(g0, g0, smc("gate_i", rows=4), None, ALU.add))
            once(dve, "g", 3, dve.tensor_scalar(g1, g1, smc("gate_f", rows=4), None, ALU.add))
            dve.scalar_tensor_tensor(x0, g1, -1.0, g1, op0=ALU.mult, op1=ALU.max).then_inc(s("g_abs"), 1)
            once(dve, "g", 4, dve.memset(x1, 0.0))
            dve.wait_ge(s("g_exp"), 2)
            once(dve, "g", 5, dve.scalar_tensor_tensor(g1, g1, 0.0, x0, op0=ALU.min, op1=ALU.subtract))
            once(dve, "g", 6, dve.tensor_copy(x0, x1))
            once(dve, "g", 7, dve.tensor_tensor_scan(out=x1, data0=g1, data1=x0, initial=0.0, op0=ALU.add, op1=ALU.add))
            once(dve, "g", 8, dve.tensor_tensor(g0, g0, x1, ALU.subtract))
            once(dve, "g", 9, dve.tensor_tensor_scan(out=g1, data0=g0, data1=x0, initial=0.0, op0=ALU.max, op1=ALU.max))
            once(dve, "g", 10, dve.tensor_scalar(x0, g1, -1.0, None, ALU.mult))
            once(dve, "g", 11, dve.scalar_tensor_tensor(x1, x1, -1.0, g1, op0=ALU.mult, op1=ALU.subtract))
            dve.wait_ge(s("c_lo"), 3)
            dve.memset(tt(0)[:, 0:4], 0.0).then_inc(s("pad"), 1)
            dve.memset(tt(1)[:, 0:4], 0.0).then_inc(s("pad"), 1)
            dve.wait_ge(s("pad"), 2)
            for j in range(8):
                q = j % 2
                if q == 0:
                    dve_lo(dve, 4 + j // 2, (j // 2) % 2)
                cb, y = tt(q), tt(2 + q, S)
                dve_take(dve, 3 + j // 2, q, S, cb[:, 4:4 + S], RX)
                dve.wait_ge(s("cv_y"), j + 1)
                for t in range(3):
                    dve.scalar_tensor_tensor(y, cb[:, 1 + t:1 + t + S], smc("conv_w", 8 * t + j), y,
                                             op0=ALU.mult, op1=ALU.add).then_inc(s("cv_acc"), 1)
                    dve.wait_ge(s("cv_acc"), 3 * j + t + 1)
                dve.wait_ge(s("cv_hi"), j + 1)
                dve.tensor_tensor(a_mqk(1, j), tt(4 + q, S), a_mqk(0, j).bitcast(f32), ALU.subtract).then_inc(s("cv_lo"), 1)

            def v_lo(g):
                dve.wait_ge(s("v_hi"), g + 1)
                dve.tensor_tensor(a_v(1, g % 4), ps[:, 3 + 4 * (g % 2), :], a_v(0, g % 4).bitcast(f32),
                                  ALU.subtract).then_inc(s("v_lo"), 1)
            dve_lo(dve, 8, 0)
            dve.wait_ge(s("cv_s"), 8)
            for hh in range(2):
                dve_take(dve, 7, hh, S, tt(hh, S), RX)
            dve_lo(dve, 9, 1)
            for hh in range(2):
                dve_take(dve, 8, hh, S, tt(2 + hh, S), RX)
            v_lo(0)
            v_lo(1)
            dve_lo(dve, 10, 0)
            for hh in range(4):
                if hh == 2:
                    v_lo(2)
                    v_lo(3)
                    dve_lo(dve, 11, 1)
                if hh >= 2:
                    dve.wait_ge(s("so"), hh - 1)
                dve_take(dve, 9 + hh // 2, hh % 2, S, tt(4 + hh % 2, S), RX)
            dve_lo(dve, 12, 0)
            dve.wait_ge(s("so"), 4)
            dve.wait_ge(s("g_tr"), 1)
            once(dve, "gc", 1, dve.tensor_copy(cols[:, 64:80], ps[:, 1, 0:16]))
            for hh in range(4):
                dve.wait_ge(s("bc"), hh + 1)
                for kb in range(4):
                    dve.tensor_tensor(tmp[:, 2560 + kb * P:2560 + kb * P + P], ps[:, 1, kb * P:kb * P + P],
                                      tri[:, :], ALU.add).then_inc(s("m_d"), 1)
                dve.wait_ge(s("m_e"), 8 * hh + 8)
                dve.wait_ge(s("m_s"), hh + 1)
                for kb in range(4):
                    b, at = [(0, 0), (2, 0), (4, 0), (2, KB_N[1])][kb]
                    e, p = KB_AT[kb], PACK + KB_AT[kb]
                    dve.scalar_tensor_tensor(tmp[:, p:p + KB_N[kb]], ps[:, b, at:at + KB_N[kb]], SCM,
                                             tmp[:, e:e + KB_N[kb]], op0=ALU.mult, op1=ALU.mult).then_inc(s("m_p"), 1)
                dve.wait_ge(s("m_hi"), hh + 1)
                dve.tensor_tensor(a_p(1), tmp[:, PACK:2 * PACK], a_p(0).bitcast(f32), ALU.subtract).then_inc(s("m_lo"), 1)
                dve.wait_ge(s("m_abs"), hh + 1)
                hs, rt = rr[:, 0, 0:S], rr[:, 1, 0:S]
                n = 6 * hh
                once(dve, "m_h", n + 1, dve.tensor_tensor(sq[:, 1, 0:S], sq[:, 1, 0:S], sq[:, 0, 0:S], ALU.max))
                once(dve, "m_h", n + 2, dve.reciprocal(sq[:, 1, 0:S], sq[:, 1, 0:S]))
                once(dve, "m_h", n + 3, dve.tensor_tensor(hs, ps[:, 6, :], sq[:, 1, 0:S], ALU.mult))
                dve.wait_ge(s("m_root"), hh + 1)
                once(dve, "m_h", n + 4, dve.reciprocal(rt, rt))
                once(dve, "m_h", n + 5, dve.scalar_tensor_tensor(hs, hs, smc("mlstm_norm", hh), rt, op0=ALU.mult, op1=ALU.mult))
                once(dve, "m_h", n + 6, dve.tensor_tensor(hs, hs, so(hh), ALU.mult))
                dve.wait_ge(s("m_zhi"), hh + 1)
                dve.tensor_tensor(z_lo[:, 4 + hh, 0:S], hs, z_hi[:, 4 + hh, 0:S].bitcast(f32), ALU.subtract).then_inc(s("m_zlo"), 1)
            def low(j, n, p, o, lo, hi):
                dve.wait_ge(s("q_hi"), n)
                dve.tensor_tensor(lo, banks(p % 2, o, S), hi.bitcast(f32), ALU.subtract).then_inc(ps_free, 1)
            for j in range(4):
                low(j, j + 1, P_UQ + j // 2, j % 2, a_q(1, j), a_q(0, j))
            for o in range(2):
                dve_take(dve, P_UQ + 2, o, S, AX[o], rope_cs[:, 0, :])
            for o in range(2):
                dve_take(dve, P_UQ + 3, o, S, tt(o, S), rope_cs[:, 1, :])
            dve.wait_ge(ps_free, 2 * (P_UQ + 4))
            for o in range(2):
                dve.tensor_tensor(AX[o], AX[o], tt(o, S), ALU.add).then_inc(s("qr_sum"), 1)
            for o in range(2):
                dve.wait_ge(s("q_hi"), 5 + o)
                dve.tensor_tensor(a_q(1, 4 + o), AX[o], a_q(0, 4 + o).bitcast(f32), ALU.subtract).then_inc(s("qr_lo"), 1)
            dve_lo(dve, 13, 1)
            for j in range(4):
                low(j, 6 + j + 1, P_UKV + j // 2, j % 2, a_k(1, j), a_k(0, j))
            for j in range(4):
                dve_take(dve, P_UKV + 2 + j // 2, j % 2, S, tt(2 + j, S))
            for g in range(4, 8):
                v_lo(g)
            dve_lo(dve, 14, 0)

            def mla_max(u):
                b, q = u % 4, u % 2
                n = P * (b + 1)
                dve.wait_ge(s("a_s"), u + 1)
                if u >= 2:
                    dve.wait_ge(s("a_tr"), u - 1)
                dve.tensor_tensor_reduce(out=tt(q, n), in0=ps[:, 4 * q, 0:n], in1=dist[:, S - n:S], scale=1.0,
                                         scalar=NEG, op0=ALU.add, op1=ALU.max, accum_out=cols[:, u:u + 1]).then_inc(s("a_max"), 1)
                dve.wait_ge(s("a_max"), u + 1)
                dve.tensor_scalar(cols[:, 16 + u:17 + u], cols[:, u:u + 1], -SC1, None, ALU.mult).then_inc(s("a_nmx"), 1)

            def mla_norm(u):
                n = P * (u % 4 + 1)
                dve.wait_ge(s("a_exp"), u + 1)
                once(dve, "a_rcp", u + 1, dve.reciprocal(cols[:, 48 + u:49 + u], cols[:, 32 + u:33 + u]))
                dve.tensor_scalar(tt(u % 2, n), tt(u % 2, n), cols[:, 48 + u:49 + u], None, ALU.mult).then_inc(s("a_norm"), 1)

            def mla_lo(u):
                n = P * (u % 4 + 1)
                dve.wait_ge(s("a_hi"), u + 1)
                dve.tensor_tensor(a_pt(1, u % 2, n), ps[:, 2 + 4 * (u % 2), 0:n], a_pt(0, u % 2, n).bitcast(f32),
                                  ALU.subtract).then_inc(s("a_lo"), 1)

            def mla_out(u):
                dve.wait_ge(s("a_zhi"), u + 1)
                hh, b = divmod(u, 4)
                dve.tensor_tensor(z_lo[:, hh, P * b:P * b + P], ps[:, 1 + 4 * (u % 2), 0:P],
                                  z_hi[:, hh, P * b:P * b + P].bitcast(f32), ALU.subtract).then_inc(s("a_zlo"), 1)
            mla_max(0)
            for u in range(18):
                if u + 1 < 16:
                    mla_max(u + 1)
                if u < 16:
                    mla_norm(u)
                if 1 <= u < 17:
                    mla_lo(u - 1)
                if u >= 2:
                    mla_out(u - 2)

            def out_tiles(b0, p0, ntok):
                for j in range(4):
                    if j or b0 != B_OUT1:
                        dve_lo(dve, b0 + j + 1, (b0 + j + 1) % 2)
                    for o in range(2):
                        dve_take(dve, p0 + j, o, ntok, ac(2 * j + o)[:, T - ntok:T])
            out_tiles(B_OUT1, P_OUT1, S)
            dve_post(dve, 0, S, META, nxt_c0=META)

            def add_acc(p, o, k, ntok):
                dve.wait_ge(ps_full, 2 * p + o + 1)
                dve.wait_ge(ps_free, 2 * p + o)
                dst = like(ac(k)[:, T - ntok:T], ntok)
                dve.tensor_tensor(dst, dst, banks(slot_of(p), o, ntok), ALU.add).then_inc(ps_free, 1)

            def slot_of(p):
                return p % 2
            done = 0
            R1 = rr[:, 0, META:T]
            for c, nt in enumerate(CHUNKS1):
                b0, p0 = B_MLP1 + done + 4 * c, P_MLP1 + done + 4 * c
                for j in range(nt):
                    dve_lo(dve, b0 + j + 1, (b0 + j + 1) % 2)
                    n = done + j
                    if n == 0:
                        dve_rstd(dve, 2, S, META)
                        dve.wait_ge(rstd, 3)
                    q = n % 2
                    dve_take(dve, p0 + j, 0, S, tt(q, S), R1)
                    dve_take(dve, p0 + j, 1, S, tt(4 + q, S), R1)
                    dve.wait_ge(s("sw_silu"), n + 1)
                    dve.wait_ge(ps_free, 2 * (p0 + j) + 2)
                    once(dve, "sw_hm", n + 1, dve.tensor_tensor(tt(4 + q, S), tt(4 + q, S), tt(2 + q, S), ALU.mult))
                    dve.wait_ge(s("sw_hi"), n + 1)
                    dve.tensor_tensor(a_hid(1, j)[:, 0:S], tt(4 + q, S), a_hid(0, j)[:, 0:S].bitcast(f32),
                                      ALU.subtract).then_inc(s("sw_lo"), 1)
                if c == 0:
                    dve.wait_ge(acc_zero, 1)
                for j in range(4):
                    dve_lo(dve, b0 + nt + j + 1, (b0 + nt + j + 1) % 2)
                    for o in range(2):
                        add_acc(p0 + nt + j, o, 2 * j + o, S)
                done += nt
            dve_post(dve, 1, S, META, nxt_c0=META)

            for k in range(2):
                dve.wait_ge(s("p_hi"), k + 1)
                dve.tensor_tensor(a_c(1, k), tmp[:, k * S:k * S + S], a_c(0, k).bitcast(f32), ALU.subtract).then_inc(s("p_lo"), 1)
            dve_lo(dve, B_PLEG, B_PLEG % 2)
            for k in range(KD):
                dve_take(dve, P_PLEP + k // 2, k % 2, S, ac(k)[:, META:T])
            for k in range(KD):
                if k % 2 == 0:
                    dve_lo(dve, B_PLEG + k // 2 + 1, (B_PLEG + k // 2 + 1) % 2)
                dve.wait_ge(s("ple_s"), k + 1)
                a = ac(k)[:, META:T]
                dve.tensor_tensor(a, a, tt(2 + k % 2, S), ALU.mult).then_inc(ps_free, 1)
                dve.wait_ge(ps_free, 2 * P_PLEG + k + 1)
                dve.tensor_tensor(h[:, k, META:T], h[:, k, META:T], a, ALU.add).then_inc(s("ple_h"), 1)
            for k in range(KD):
                dve_zlo(dve, 3, k, 0)

            nb = 0

            def d_max(u):
                nonlocal nb
                head, b = divmod(u, 5)
                if b == 0:
                    slope = 2.0 ** (-8.0 * (head + 1) / DIFF_HEADS)
                    dve.tensor_scalar(tt(4), dist[:, :], slope / SC2, None, ALU.mult).then_inc(s("d_bias"), 1)
                    dve.wait_ge(s("d_bias"), head + 1)
                off = S - P if b == 0 else S - P * b
                off = S - P + META if b == 0 else S - P * b
                for c in range(2):
                    nq, nk, t = unit(u, c)
                    w = (u % 2) * 2 + c
                    dve.wait_ge(s("d_s"), 2 * u + c + 1)
                    if u >= 2 and c == 0:
                        dve.wait_ge(s("d_tr"), u - 1)
                    bi = tt(4)[0:nq, off:off + nk] if b == 0 else tt(4)[0:nq, off:off + nk]
                    dve.tensor_tensor_reduce(out=like(t, nk), in0=ps[0:nq, 2 * c, 0:nk] if nk <= 512 else ps[0:nq, 2 * c:2 * c + 2, 0:HALF],
                                             in1=like(bi, nk), scale=1.0, scalar=NEG, op0=ALU.add, op1=ALU.max,
                                             accum_out=cols[0:nq, 90 + w:91 + w]).then_inc(s("d_max"), 1)
                    dve.wait_ge(s("d_max"), 2 * u + c + 1)
                    dve.tensor_scalar(cols[0:nq, 94 + w:95 + w], cols[0:nq, 90 + w:91 + w], -SC2, None,
                                      ALU.mult).then_inc(s("d_nmx"), 1)

            def d_mix(u):
                nq, nk, t0 = unit(u, 0)
                t1 = unit(u, 1)[2]
                w = (u % 2) * 2
                dve.wait_ge(s("d_exp"), 2 * u + 2)
                once(dve, "d_rc", 2 * u + 1, dve.reciprocal(cols[0:nq, 102 + w:104 + w], cols[0:nq, 98 + w:100 + w]))
                once(dve, "d_rc", 2 * u + 2, dve.tensor_tensor(cols[0:nq, 103 + w:104 + w], cols[0:nq, 103 + w:104 + w],
                                                               cols[0:nq, 84:85], ALU.mult))
                once(dve, "d_m1", u + 1, dve.tensor_scalar(t1, t1, cols[0:nq, 103 + w:104 + w], None, ALU.mult))
                dve.scalar_tensor_tensor(t0, t0, cols[0:nq, 102 + w:103 + w], t1, op0=ALU.mult, op1=ALU.add).then_inc(s("d_a"), 1)

            def d_lo(u):
                nq, nk, _ = unit(u, 0)
                dve.wait_ge(s("d_hi"), d_parts(u))
                dve.tensor_tensor(a_dpt(1, u % 2, 0, META)[:, 0:nq], ps[0:META, 6 + u % 2, 0:nq],
                                  a_dpt(0, u % 2, 0, META)[:, 0:nq].bitcast(f32), ALU.subtract).then_inc(s("d_lo"), 1)
                if nk > META:
                    nt = (nk - META) // P
                    dve.tensor_tensor(a_dpt(1, u % 2, 1, P, nt), ps[:, 4 + u % 2, 0:nk - META],
                                      a_dpt(0, u % 2, 1, P, nt).bitcast(f32), ALU.subtract).then_inc(s("d_lo"), 1)

            def d_out(u):
                head, b = divmod(u, 5)
                nq = unit(u, 0)[0]
                q0 = 0 if b == 0 else META + P * (b - 1)
                dve.wait_ge(s("d_pv"), u + 1)
                dve.tensor_copy(ac(head)[:, q0:q0 + nq], ps[:, 6 + u % 2, P:P + nq]).then_inc(s("d_o"), 1)

            for g in range(GROUPS):
                b0, p0 = B_QKV + 3 * g, P_QKV + 3 * g
                for i in range(2):
                    dve_lo(dve, b0 + i + 1, (b0 + i + 1) % 2)
                    if g == 0 and i == 0:
                        dve_rstd(dve, 4, T, 0)
                        dve.wait_ge(rstd, 5)
                    for o in range(2):
                        dve_take(dve, p0 + i, o, T, tt(2 * i + o), rr[:, 0, :])
                    for o in range(2):
                        dve.wait_ge(s("dq_hi"), 4 * g + 2 * i + o + 1)
                        dve.tensor_tensor(a_qk(1, o, i), tt(2 * i + o), a_qk(0, o, i).bitcast(f32),
                                          ALU.subtract).then_inc(s("dq_lo"), 1)
                dve_lo(dve, b0 + 3, (b0 + 3) % 2)
                for i in range(2):
                    dve_take(dve, p0 + 2, i, T, tt(4 + i), rr[:, 0, :])
                for i in range(2):
                    dve.wait_ge(s("dv_hi"), 4 * g + 2 * i + 2)
                    dve.tensor_tensor(a_dv(1, i, 1, P, 4), ps[:, 4 + i, :], a_dv(0, i, 1, P, 4).bitcast(f32),
                                      ALU.subtract).then_inc(s("dv_lo"), 1)
                    dve.tensor_tensor(a_dv(1, i, 0, META), ps[0:META, 6 + i, 0:P], a_dv(0, i, 0, META).bitcast(f32),
                                      ALU.subtract).then_inc(s("dv_lo"), 1)
                if g == 0:
                    dve.wait_ge(s("dist"), 2)
                first = UG * g
                d_max(first)
                for u in range(first, first + UG + 2):
                    if u + 1 < first + UG:
                        d_max(u + 1)
                    if u < first + UG:
                        d_mix(u)
                    if first < u <= first + UG:
                        d_lo(u - 1)
                    if u >= first + 2:
                        d_out(u - 2)
                for i in range(2):
                    k = 2 * g + i
                    dve.wait_ge(s("d_root"), k + 1)
                    once(dve, "d_n", 2 * k + 1, dve.reciprocal(rr[:, 1, :], rr[:, 1, :]))
                    once(dve, "d_n", 2 * k + 2, dve.scalar_tensor_tensor(ac(k), ac(k), smc("subln"), rr[:, 1, :],
                                                                         op0=ALU.mult, op1=ALU.mult))
                    dve.wait_ge(s("d_ohi"), k + 1)
                    dve.tensor_tensor(a_out(1, k), ac(k), a_out(0, k).bitcast(f32), ALU.subtract).then_inc(s("d_olo"), 1)
            out_tiles(B_OUT2, P_OUT2, T)
            dve_post(dve, 2, T, 0, nxt_c0=0)

            def dve_mlp(l, b0, p0, si, ntok):
                r = rr[:, 0, T - ntok:T]

                def chunk(c, last=False):
                    head = isinstance(c, int) and c == 0
                    for j in range(KD // 2):
                        dve_lo(dve, b0 + j + 1 + 8 * c, (b0 + j + 1) % 2)
                        if head and j == 0:
                            dve_rstd(dve, si, ntok, T - ntok)
                            dve.wait_ge(rstd, si + 1)
                        for o in range(2):
                            n = 2 * (p0 + j) + o + 1 + 16 * c
                            dve.wait_ge(ps_full, n)
                            dve.scalar_tensor_tensor(like(tt(o, ntok), ntok), banks((p0 + j) % 2, o, ntok), 0.0,
                                                     like(r, ntok), op0=ALU.max, op1=ALU.mult).then_inc(ps_free, 1)
                        for o in range(2):
                            n = FF2 * l + 2 * j + o + 8 * c
                            dve.wait_ge(s("hid_hi"), n + 1)
                            dve.tensor_tensor(a_hid(1, 2 * j + o)[:, 0:ntok], tt(2 + o, ntok),
                                              a_hid(0, 2 * j + o)[:, 0:ntok].bitcast(f32), ALU.subtract).then_inc(s("hid_lo"), 1)
                    if head:
                        dve.wait_ge(acc_zero, 2 + l)
                    for j in range(4, 8):
                        if not (last and j == 7):
                            dve_lo(dve, b0 + j + 1 + 8 * c, (b0 + j + 1) % 2)
                        for o in range(2):
                            n = 2 * (p0 + j) + o + 16 * c
                            dve.wait_ge(ps_full, n + 1)
                            dve.wait_ge(ps_free, n)
                            dst = like(ac(2 * (j - 4) + o)[:, T - ntok:T], ntok)
                            dve.tensor_tensor(dst, dst, banks((p0 + j) % 2, o, ntok), ALU.add).then_inc(ps_free, 1)
                return chunk
            mlp = dve_mlp(0, B_MLP2, P_MLP2, 6, T)
            mlp(0)
            with dve.Fori(1, NCH2) as c:
                mlp(c)
            dve_post(dve, 3, T, 0, nxt_c0=0)
            for m in range(4):
                b0, p0 = B_CONV + 3 * m, P_CONV + 3 * m
                for i in range(2):
                    dve_lo(dve, b0 + i + 1, (b0 + i + 1) % 2)
                    if m == 0 and i == 0:
                        dve_rstd(dve, 8, T, 0)
                        dve.wait_ge(rstd, 9)
                    j = 2 * m + i
                    if j >= 2:
                        dve.wait_ge(s("sc_lo"), 2 * m)
                    dve_take(dve, p0 + i, 0, T, tt(0), rr[:, 0, :])
                    dve_take(dve, p0 + i, 1, T, tt(1), rr[:, 0, :])
                    dve.wait_ge(ps_free, 2 * (p0 + i) + 2)
                    once(dve, "sc_v", j + 1, dve.tensor_tensor(tt(2 + i), tt(0), tt(1), ALU.mult))
                    dve.wait_ge(s("sc_y"), j + 1)
                    for t in range(2):
                        once(dve, "sc_acc", 2 * j + t + 1, dve.scalar_tensor_tensor(
                            tt(4 + i, S), tt(2 + i)[:, META - 2 + t:T - 2 + t], smc("conv2_w", 8 * t + j), tt(4 + i, S),
                            op0=ALU.mult, op1=ALU.add))
                dve_lo(dve, b0 + 3, (b0 + 3) % 2)
                for i in range(2):
                    j = 2 * m + i
                    dve.wait_ge(ps_full, 2 * (p0 + 2) + i + 1)
                    b = 4 * ((p0 + 2) % 2) + 2 * i
                    dve.tensor_tensor(like(tt(i), T), banks((p0 + 2) % 2, i, T), like(rr[:, 0, :], T), ALU.mult).then_inc(ps_free, 1)
                    dve.wait_ge(ps_free, 2 * (p0 + 2) + i + 1)
                    once(dve, "sc_o", j + 1, dve.tensor_tensor(tt(i, S), tt(i)[:, META:T], tt(4 + i, S), ALU.mult))
                for i in range(2):
                    j = 2 * m + i
                    dve.wait_ge(s("sc_hi"), j + 1)
                    dve.tensor_tensor(a_out(1, j, 0, S), tt(i, S), a_out(0, j, 0, S).bitcast(f32), ALU.subtract).then_inc(s("sc_lo"), 1)
            out_tiles(B_OUT3, P_OUT3, S)
            dve_post(dve, 4, S, META, nxt_c0=META)
            mlp = dve_mlp(1, B_MLP3, P_MLP3, 10, S)
            mlp(0)
            with dve.Fori(1, NCH2 - 1) as c:
                mlp(c)
            mlp(NCH2 - 1, last=True)
            dve_post(dve, 5, S, META)

        @block.tensor
        def _(pe):
            def three(dst, lh, rh, start, stop):
                pe.matmul(dst, lh(0), rh(0), start=start, stop=False)
                pe.matmul(dst, lh(0), rh(1), start=False, stop=False)
                return pe.matmul(dst, lh(1), rh(0), start=False, stop=stop)

            def gemm(b, ntok=S, z=z_part, nk=KD, z_ready=None, sub=0, p=None):
                p = pair_of(b) + sub if p is None else p
                pe.wait_ge(wlo, b + 1)
                project(pe, b % 2, p % 2, 2 * sub, nk, z, ntok, 2 * (p - 1) if p >= 2 else None, z_ready)

            def stat_after(b, si, ntok, c0):
                pe_stat(pe, si, (pair_of(b) + 1) % 2, ntok, c0)
                pe.wait_ge(rooted, si + 1)
            pe.wait_ge(consts, 16)
            gemm(0, z_ready=z_ready_for(pe, 0))
            stat_after(0, 0, S, META)
            gemm(1)
            gemm(2)
            pe.wait_ge(s("c_sq"), 3)
            for k in range(2):
                last = pe.matmul(ps[:, 3, :], ones[:, :], tt(3 + k, S), start=(k == 0), stop=(k == 1))
            last.then_inc(s("c_stat"), 1)
            pe.matmul(ps[:, 7, :], ones[:, :], tt(5, S), start=True, stop=True).then_inc(s("c_stat"), 1)
            for b in range(3, 9):
                gemm(b)

            def v_transpose(g, src):
                if g >= 2:
                    pe.wait_ge(s("v_lo"), g - 1)
                for t in range(4):
                    last = pe.transpose(ps[:, 3 + 4 * (g % 2), t * P:t * P + P], src[:, t * P:t * P + P], ident[:, :])
                last.then_inc(s("v_tr"), 1)
            pe.wait_ge(s("c_root"), 2)
            pe.wait_ge(ps_free, 2 * 8)
            v_transpose(0, tt(0, S))
            v_transpose(1, tt(1, S))
            gemm(9)
            pe.wait_ge(ps_free, 2 * 9)
            v_transpose(2, tt(2, S))
            v_transpose(3, tt(3, S))
            gemm(10)
            pe.wait_ge(s("g"), 11)
            for t in range(4):
                last = pe.transpose(ps[:, 1, 4 * t:4 * t + 4], G0[0:4, t * P:t * P + P], ident[0:4, 0:4])
            last.then_inc(s("g_tr"), 1)
            pe.wait_ge(s("sel"), 2)
            pe.wait_ge(ps_free, 2 * 11)
            pe.wait_ge(s("cv_lo"), 8)
            pe.wait_ge(s("v_lo"), 4)
            for hh in range(4):
                sel = ssum[0:4, hh * P:hh * P + P]
                pe.wait_ge(s("gc"), 1)
                if hh:
                    pe.wait_ge(s("m_e"), 8 * hh)
                    pe.wait_ge(s("m_d"), 4 * hh)
                pe.matmul(ps[:, 1, :], sel, AX[0][0:4, :], start=True, stop=True)
                pe.matmul(ps[:, 5, :], sel, AX[1][0:4, :], start=True, stop=True).then_inc(s("bc"), 1)
                if hh:
                    pe.wait_ge(s("m_p"), 4 * hh)
                for kb in range(4):
                    b, at = [(0, 0), (2, 0), (4, 0), (2, KB_N[1])][kb]
                    last = three(ps[:, b, at:at + KB_N[kb]], lambda x: a_mqk(x, 4 + hh)[:, kb * P:kb * P + P],
                                 lambda x: a_mqk(x, hh)[:, kb * P:S], True, True)
                last.then_inc(s("m_s"), 1)
                pe.wait_ge(s("m_lo"), hh + 1)
                if hh:
                    pe.wait_ge(s("m_h"), 6 * hh)
                for kb in range(4):
                    three(ps[:, 6, kb * P:S], lambda x: a_v(x, hh)[:, kb * P:kb * P + P],
                          lambda x: a_p(x, KB_AT[kb], KB_N[kb]), kb == 0, kb == 3)
                for kb in range(4):
                    pe.matmul(ps[:, 7, kb * P:S], ones_r[:, :], a_p(0, KB_AT[kb], KB_N[kb]), start=(kb == 0), stop=False)
                    last = pe.matmul(ps[:, 7, kb * P:S], ones_r[:, :], a_p(1, KB_AT[kb], KB_N[kb]), start=False, stop=(kb == 3))
                last.then_inc(s("m_nd"), 1)
                pe.wait_ge(s("m_sq"), hh + 1)
                pe.matmul(ps[:, 3, :], ones[:, :], rr[:, 1, 0:S], start=True, stop=True).then_inc(s("m_st"), 1)

            def c_part(x, k):
                return a_c(x, k)

            def ckv_part(x, k):
                return a_c(x, 2)
            pe.wait_ge(s("m_h"), 24)
            for sub in range(4):
                gemm(B_UQ, z=c_part, nk=2, sub=sub)
            for sub in range(4):
                gemm(B_UKV, z=ckv_part, nk=1, sub=sub)
            for g in range(4, 8):
                pe.wait_ge(ps_free, 2 * (P_UKV + 2) + g - 4 + 1)
                pe.wait_ge(s("v_lo"), g - 1)
                if g == 4:
                    pe.wait_ge(s("m_root"), 4)
                for t in range(4):
                    last = pe.transpose(ps[:, 3 + 4 * (g % 2), t * P:t * P + P], tt(2 + g - 4, S)[:, t * P:t * P + P], ident[:, :])
                last.then_inc(s("v_tr"), 1)
            pe.wait_ge(s("v_lo"), 8)
            pe.wait_ge(s("qr_lo"), 2)
            pe.wait_ge(ps_free, 2 * (P_UKV + 4))

            def mla_s(u):
                hh, b = divmod(u, 4)
                n = P * (b + 1)
                if u >= 2:
                    pe.wait_ge(s("a_max"), u - 1)
                dst = ps[:, 4 * (u % 2), 0:n]
                three(dst, lambda x: a_q(x, hh)[:, b * P:b * P + P], lambda x: a_k(x, hh)[:, 0:n], True, False)
                three(dst, lambda x: a_q(x, 4 + hh // 2)[:, b * P:b * P + P], lambda x: a_kpe(x, hh % 2)[:, 0:n],
                      False, True).then_inc(s("a_s"), 1)

            def mla_t(u):
                pe.wait_ge(s("a_norm"), u + 1)
                if u >= 2:
                    pe.wait_ge(s("a_lo"), u - 1)
                for kb in range(u % 4 + 1):
                    last = pe.transpose(ps[:, 2 + 4 * (u % 2), kb * P:kb * P + P], tt(u % 2)[:, kb * P:kb * P + P], ident[:, :])
                last.then_inc(s("a_tr"), 1)

            def mla_pv(u):
                hh = u // 4
                pe.wait_ge(s("a_lo"), u + 1)
                if u >= 2:
                    pe.wait_ge(s("a_zlo"), u - 1)
                for kb in range(u % 4 + 1):
                    last = three(ps[:, 1 + 4 * (u % 2), 0:P], lambda x: a_v(x, hh)[:, kb * P:kb * P + P],
                                 lambda x: a_pt(x, u % 2)[:, kb * P:kb * P + P], kb == 0, kb == u % 4)
                last.then_inc(s("a_pv"), 1)
            mla_s(0)
            mla_s(1)
            for u in range(17):
                if u < 16:
                    mla_t(u)
                if u + 2 < 16:
                    mla_s(u + 2)
                if u >= 1:
                    mla_pv(u - 1)
            pe.wait_ge(s("a_zlo"), 16)
            pe.wait_ge(s("m_zlo"), 4)
            for j in range(4):
                gemm(B_OUT1 + j)
            pe_stat(pe, 1, 0, S, META)

            def hid_part(x, k):
                return a_hid(x, k)
            done = 0
            for c, nt in enumerate(CHUNKS1):
                b0 = B_MLP1 + done + 4 * c
                for j in range(nt):
                    first = done + j == 0
                    gemm(b0 + j, z_ready=z_ready_for(pe, 1) if first else None)
                    if first:
                        stat_after(b0, 2, S, META)
                for j in range(4):
                    gemm(b0 + nt + j, z=hid_part, nk=nt, z_ready=(lambda k: pe.wait_ge(s("sw_lo"), done + k + 1)) if j == 0 else None)
                done += nt
            pe_stat(pe, 3, 0, S, META)
            pe.wait_ge(s("p_lo"), 2)
            pe.wait_ge(rooted, 4)
            for sub in range(4):
                gemm(B_PLEP, z=c_part, nk=2, sub=sub)
            for j in range(4):
                gemm(B_PLEG + j, z_ready=z_ready_for(pe, 2) if j == 0 else None)

            def d_s(u):
                i, b = (u // 5) % 2, u % 5
                nq, nk, _ = unit(u, 0)
                q0 = 0 if b == 0 else META + P * (b - 1)
                for c in range(2):
                    r = slice(64 * c, 64 * c + 64)
                    if u % UG >= 1:
                        pe.wait_ge(s("d_max"), 2 * (u - 1) + c + 1)
                    for cut, (a, e) in enumerate([(0, nk)] if nk <= 512 else [(0, HALF), (HALF, T)]):
                        last = three(ps[:, 2 * c + cut, 0:e - a], lambda x: a_qk(x, 0, i)[r, q0:q0 + P],
                                     lambda x: a_qk(x, 1, i)[r, a:e], True, True)
                    last.then_inc(s("d_s"), 1)

            def d_t(u):
                nq, nk, t = unit(u, 0)
                pe.wait_ge(s("d_a"), u + 1)
                if u % UG >= 2:
                    pe.wait_ge(s("d_lo"), d_parts(u - 2))
                    pe.wait_ge(s("d_o"), u - 1)
                last = pe.transpose(ps[0:META, 6 + u % 2, 0:nq], t[:, 0:META], ident[0:nq, 0:nq])
                for kb in range((nk - META) // P):
                    last = pe.transpose(ps[:, 4 + u % 2, kb * P:kb * P + P], t[:, META + kb * P:META + kb * P + P], ident[:, :])
                last.then_inc(s("d_tr"), 1)

            def d_pv(u):
                i = (u // 5) % 2
                nq, nk, _ = unit(u, 0)
                pe.wait_ge(s("d_lo"), d_parts(u))
                dst = ps[:, 6 + u % 2, P:P + nq]
                nt = (nk - META) // P
                last = three(dst, lambda x: a_dv(x, i, 0, META), lambda x: a_dpt(x, u % 2, 0, META)[:, 0:nq], True, nt == 0)
                for t in range(1, nt + 1):
                    last = three(dst, lambda x: a_dv(x, i, t), lambda x: a_dpt(x, u % 2, t), False, t == nt)
                last.then_inc(s("d_pv"), 1)

            for g in range(GROUPS):
                b0, p0 = B_QKV + 3 * g, P_QKV + 3 * g
                if g:
                    pe.wait_ge(s("d_root"), 2 * g)
                gemm(b0, T, z_ready=z_ready_for(pe, 3) if g == 0 else None)
                if g == 0:
                    stat_after(b0, 4, T, 0)
                gemm(b0 + 1, T)
                gemm(b0 + 2, T)
                pe.wait_ge(ps_free, 2 * (p0 + 3))
                for i in range(2):
                    for t in range(4):
                        pe.transpose(ps[:, 4 + i, t * P:t * P + P], tt(4 + i)[:, META + t * P:META + t * P + P], ident[:, :])
                    pe.transpose(ps[0:META, 6 + i, 0:P], tt(4 + i)[:, 0:META], ident[:, :]).then_inc(s("dv_tr"), 1)
                pe.wait_ge(s("dq_lo"), 4 * g + 4)
                pe.wait_ge(s("dv_lo"), 4 * g + 4)
                first = UG * g
                d_s(first)
                d_s(first + 1)
                for u in range(first, first + UG + 1):
                    if u < first + UG:
                        d_t(u)
                    if u + 2 < first + UG:
                        d_s(u + 2)
                    if u > first:
                        d_pv(u - 1)
                for i in range(2):
                    pe.wait_ge(s("d_sq"), 2 * g + i + 1)
                    for c in range(2):
                        last = pe.matmul(ps[:, 2 * i + c, 0:HALF], ones[:, :], sq[:, i, c * HALF:(c + 1) * HALF], start=True, stop=True)
                    last.then_inc(s("d_st"), 1)

            def out_part(x, k):
                return a_out(x, k)
            pe.wait_ge(s("d_olo"), 8)
            pe.wait_ge(s("d_o"), UG * GROUPS)
            for j in range(4):
                gemm(B_OUT2 + j, T, z=out_part)
            pe_stat(pe, 5, 0, T, 0)

            def pe_mlp(l, b0, p0, zi, si, ntok):
                def chunk(c):
                    head = isinstance(c, int) and c == 0
                    for j in range(8):
                        pe.wait_ge(wlo, b0 + j + 1 + 8 * c)
                        if head and j == 1:
                            pe.wait_ge(rooted, si + 1)
                        if j < 4:
                            ready = z_ready_for(pe, zi) if head and j == 0 else None
                        else:
                            ready = (lambda k: pe.wait_ge(s("hid_lo"), FF2 * l + k + 1 + 8 * c)) if j == 4 else None
                        project(pe, (b0 + j) % 2, (p0 + j) % 2, 0, KD, z_part if j < 4 else hid_part, ntok,
                                2 * (p0 + j - 1) + 16 * c, ready)
                        if head and j == 0:
                            pe_stat(pe, si, (p0 + 1) % 2, ntok, T - ntok)
                return chunk
            mlp = pe_mlp(0, B_MLP2, P_MLP2, 4, 6, T)
            mlp(0)
            with pe.Fori(1, NCH2) as c:
                mlp(c)
            pe_stat(pe, 7, 0, T, 0)
            for j in range(12):
                gemm(B_CONV + j, T, z_ready=z_ready_for(pe, 5) if j == 0 else None)
                if j == 0:
                    stat_after(B_CONV, 8, T, 0)
            for j in range(4):
                gemm(B_OUT3 + j, S, z=out_part, z_ready=(lambda k: pe.wait_ge(s("sc_lo"), k + 1)) if j == 0 else None)
            pe_stat(pe, 9, 0, S, META)
            mlp = pe_mlp(1, B_MLP3, P_MLP3, 6, 10, S)
            mlp(0)
            with pe.Fori(1, NCH2) as c:
                mlp(c)
            pe_stat(pe, 11, 0, S, META)


def pack_weights(w_in, w_uq, w_ukv, w_out, w_gate, w_up, w_down, w_ple_proj, w_ple_gate, w_in_2, w_out_2, w_up_2, w_down_2):
    stream = np.zeros((NBLK, P, BLK), np.float32)
    n = 0

    def block(*tiles):
        nonlocal n
        at = 0
        for t in tiles:
            k = t.shape[0] // P
            stream[n, :, at:at + k * P] = t.reshape(k, P, P).transpose(1, 0, 2).reshape(P, k * P)
            at += k * P
        n += 1

    def col(w, c):
        return w[:, c:c + P]
    CKV, KR, MQ, MK, MV, MO, MI, MF = 256, 384, 448, 960, 1472, 1984, 2496, 2500
    block(col(w_in, 0), col(w_in, P))
    gates = np.zeros((D, P), np.float32)
    gates[:, 0:4], gates[:, 32:36] = w_in[:, MI:MI + 4], w_in[:, MF:MF + 4]
    block(col(w_in, CKV), gates)
    t1, t2 = w_in[:, KR:KR + 32], w_in[:, KR + 32:KR + 64]
    block(np.concatenate([t1, t2, t1, t2], 1), np.concatenate([t2, t1, t2, t1], 1))
    for base in (MQ, MK, MV, MO):
        for j in range(0, 4, 2):
            block(col(w_in, base + j * P), col(w_in, base + (j + 1) * P))
    q = [w_uq[:, QKD * i:QKD * (i + 1)] for i in range(4)]
    pe = [x[:, 128:192] for x in q]
    swap = [np.concatenate([x[:, 32:64], x[:, 0:32]], 1) for x in pe]
    block(*[x[:, 0:P] for x in q], np.concatenate(pe[0:2], 1), np.concatenate(pe[2:4], 1),
          np.concatenate(swap[0:2], 1), np.concatenate(swap[2:4], 1))
    block(*[col(w_ukv, 256 * i) for i in range(4)], *[col(w_ukv, 256 * i + P) for i in range(4)])

    def columns(w):
        for j in range(0, w.shape[1] // P, 2):
            block(col(w, j * P), col(w, (j + 1) * P))
    columns(w_out)
    done = 0
    for nt in CHUNKS1:
        for j in range(done, done + nt):
            block(col(w_gate, j * P), col(w_up, j * P))
        columns(w_down[done * P:(done + nt) * P])
        done += nt
    block(*[col(w_ple_proj, j * P) for j in range(KD)])
    columns(w_ple_gate)
    for g in range(GROUPS):
        for i in range(2):
            block(col(w_in_2[0], (2 * g + i) * P), col(w_in_2[0], D + (2 * g + i) * P))
        block(col(w_in_2[0], 2 * D + 2 * g * P), col(w_in_2[0], 2 * D + (2 * g + 1) * P))
    columns(w_out_2[0])

    def mlp(up, down):
        for c in range(NCH2):
            columns(up[:, c * D:(c + 1) * D])
            columns(down[c * D:(c + 1) * D])
    mlp(w_up_2[0], w_down_2[0])
    for m in range(4):
        for i in range(2):
            block(col(w_in_2[1], D + (2 * m + i) * P), col(w_in_2[1], 2 * D + (2 * m + i) * P))
        block(col(w_in_2[1], 2 * m * P), col(w_in_2[1], (2 * m + 1) * P))
    columns(w_out_2[1])
    mlp(w_up_2[1], w_down_2[1])
    assert n == NBLK
    return stream


def tiles(v):
    v = np.asarray(v, np.float32)
    v = v.reshape(-1, v.shape[-1] // P, P)
    return v.transpose(2, 0, 1).reshape(P, -1)


def pack_small(i):
    small = np.zeros((P, NSMALL), np.float32)

    def put(name, a):
        small[0:a.shape[0], SMALL[name]:SMALL[name] + a.shape[1]] = a
    for name, key in [("attn_pre", "attn_pre_norm"), ("attn_post", "attn_post_norm"), ("ffn_pre", "ffn_pre_norm"),
                      ("ffn_post", "ffn_post_norm"), ("q_norm", "q_norm"), ("kv_norm", "kv_norm"), ("conv_b", "conv_b"),
                      ("mlstm_norm", "mlstm_norm"), ("norm2", "norm_g_2"), ("conv_w", "conv_w"), ("conv2_w", "conv_w_2"),
                      ("subln", "subln_g_2")]:
        put(name, tiles(i[key]))
    put("gate_i", np.asarray(i["gate_bias_i"]).reshape(4, 1))
    put("gate_f", np.asarray(i["gate_bias_f"]).reshape(4, 1))
    f = (np.float32(10000.0) ** (-np.arange(0, 64, 2, dtype=np.float32) / np.float32(64))).astype(np.float32)
    put("freq", np.tile(f, 4).reshape(P, 1))
    put("sfreq", np.tile(np.concatenate([-f, f]), 2).reshape(P, 1))
    return small


def host_arrays(i):
    i = {k: np.asarray(v) for k, v in i.items()}
    return {
        "wstream": pack_weights(i["w_in"][0], i["w_uq"][0], i["w_ukv"][0], i["w_out"][0], i["w_gate"][0], i["w_up"][0],
                                i["w_down"][0], i["w_ple_proj"][0], i["w_ple_gate"][0], i["w_in_2"], i["w_out_2"],
                                i["w_up_2"], i["w_down_2"]),
        "xT": np.ascontiguousarray(i["x"].reshape(S, KD, P).transpose(1, 2, 0)),
        "metaT": np.ascontiguousarray(i["meta_tokens_2"].reshape(META, KD, P).transpose(2, 1, 0)),
        "pT": np.ascontiguousarray(i["p"].reshape(S, 2, P).transpose(2, 1, 0)).reshape(P, 2 * S),
        "pos": np.ascontiguousarray(np.broadcast_to(i["positions"].reshape(1, S), (P, S))),
        "small": pack_small(i),
        "lam": np.ascontiguousarray(np.broadcast_to(i["lambda_params_2"].reshape(1, 256), (P, 256))),
    }


def kernel(**inputs):
    import concourse.bacc as bacc
    from concourse.bass_utils import run_bass_kernel_spmd

    nc = bacc.Bacc("TRN2", target_bir_lowering=False, num_devices=1, dynamic_dma_scratch_size=256)
    arrays = host_arrays(inputs)
    args = {n: nc.dram_tensor(n, a.shape, mybir.dt.from_np(a.dtype), kind="ExternalInput").ap() for n, a in arrays.items()}
    out = nc.dram_tensor("out", (KD, P, S), mybir.dt.float32, kind="ExternalOutput").ap()
    build(nc, out=out, **args)
    r = run_bass_kernel_spmd(nc, [arrays], core_ids=[0])
    y = r.results[0]["out"]
    return np.ascontiguousarray(np.asarray(y).transpose(2, 0, 1).reshape(1, S, D))
```

```python
import math

import numpy as np

import concourse.bass as bass
from concourse import mybir
from contextlib import ExitStack

P = 128
D = 1024
KD = D // P
S = 512
META = 16
T = S + META
HALF = T // 2
BLK = 2 * KD * P
QKD = 192
FF1 = 2816 // P
CHUNKS1 = [8, 8, 6]
FF2 = 4096 // P
NCH2 = FF2 // KD
DIFF_HEADS = 8
GROUPS = 4
LAM_INIT = 0.8 - 0.6 * math.exp(-0.3 * 0)
EPS = 1e-6
NEG = -1e30

B_IN, B_UQ, B_UKV, B_OUT1, B_MLP1 = 0, 11, 12, 13, 17
B_PLEP = B_MLP1 + FF1 + 4 * len(CHUNKS1)
B_PLEG = B_PLEP + 1
B_QKV = B_PLEG + 4
B_OUT2 = B_QKV + 3 * GROUPS
B_MLP2 = B_OUT2 + 4
B_CONV = B_MLP2 + 8 * NCH2
B_OUT3 = B_CONV + 12
B_MLP3 = B_OUT3 + 4
NBLK = B_MLP3 + 8 * NCH2
MANY = {B_UQ: 4, B_UKV: 4, B_PLEP: 4}


def pair_of(block):
    return block + sum(n - 1 for b, n in MANY.items() if b < block)


SMALL = {}
NSMALL = 0
for _name, _n in [("attn_pre", 8), ("attn_post", 8), ("ffn_pre", 8), ("ffn_post", 8), ("norm2", 64),
                  ("q_norm", 2), ("kv_norm", 1), ("conv_b", 8), ("conv_w", 32), ("conv2_w", 24),
                  ("mlstm_norm", 4), ("subln", 1), ("gate_i", 1), ("gate_f", 1),
                  ("freq", 1), ("sfreq", 1)]:
    SMALL[_name] = NSMALL
    NSMALL += _n

KB_N = [S - P * kb for kb in range(4)]
KB_AT = [sum(KB_N[:kb]) for kb in range(4)]
PACK = sum(KB_N)


def build(nc, wstream, xT, metaT, pT, pos, small, lam, out):
    f32, f32r, i32 = mybir.dt.float32, mybir.dt.float32r, mybir.dt.int32
    ALU, ACT = mybir.AluOpType, mybir.ActivationFunctionType
    ctx = ExitStack()
    with ctx:
        def sb(name, shape, dt=f32):
            return ctx.enter_context(nc.sbuf_tensor(name, shape, dt))

        def sem(name):
            return ctx.enter_context(nc.semaphore(name))

        w_raw = sb("w_raw", [P, 2, BLK])
        w_hi = sb("w_hi", [P, 2, BLK], f32r)
        w_lo = sb("w_lo", [P, 2, BLK], f32r)
        h = sb("h", [P, KD, T])
        z_hi = sb("z_hi", [P, KD, T], f32r)
        z_lo = sb("z_lo", [P, KD, T], f32r)
        ARENA = 3072 + 2048 + 12288 + 4 * S
        arena = sb("arena", [P, ARENA], f32r)
        acc = sb("acc", [P, KD * T])
        tmp = sb("tmp", [P, 6 * T])
        sq = sb("sq", [P, 2, T])
        ssum = sb("ssum", [P, T])
        rr = sb("rr", [P, 2, T])
        rope_cs = sb("rope_cs", [P, 2, S])
        dist = sb("dist", [P, T])
        tri = sb("tri", [P, P])
        ident = sb("ident", [P, P])
        ones = sb("ones", [P, P])
        ones_r = sb("ones_r", [P, P], f32r)
        sm = sb("sm", [P, NSMALL])
        cols = sb("cols", [P, 120])
        eps = sb("eps", [P, 4])

        ps = ctx.enter_context(nc.psum_tensor("ps", [P, 8, 512], f32))

        def smc(name, k=0, n=1, rows=P):
            return sm[0:rows, SMALL[name] + k:SMALL[name] + k + n]

        def tt(k, n=T, rows=P):
            return tmp[0:rows, k * T:k * T + n]

        def ac(k, n=T):
            return acc[:, k * T:k * T + n]

        def a_c(part, k):
            return arena[:, part * 1536 + k * S:part * 1536 + k * S + S]

        def a_kpe(part, odd, r0=0, r1=P):
            at = 3072 + (part * 2 + odd) * S
            return arena[r0:r1, at:at + S]

        A_U = 5120

        def a_mqk(part, j):
            at = A_U + (part * 8 + j) * S
            return arena[:, at:at + S]

        def a_v(part, hh):
            at = A_U + 8192 + (part * 4 + hh) * S
            return arena[:, at:at + S]

        def a_p(part, at=0, n=PACK):
            z = (z_hi if part == 0 else z_lo)[:, :, :].rearrange("p a b -> p (a b)")
            return z[:, at:at + n]

        def a_q(part, j):
            at = A_U + (part * 6 + j) * S
            return arena[:, at:at + S]

        def a_k(part, hh):
            j = part * 4 + hh
            at = A_U + 6144 + j * S if j < 4 else A_U + 12288 + (j - 4) * S
            return arena[:, at:at + S]

        def a_pt(part, slot, n=S, at=0):
            at += (part * 2 + slot) * (S + P) + P
            return arena[:, at:at + n]

        def a_ple(part, k):
            at = 2 * KD * T + (part * 2 + k) * S
            return arena[:, at:at + S]

        def a_out(part, k, c0=0, c1=T):
            at = (part * KD + k) * T
            return arena[:, at + c0:at + c1]
        A_2 = 2 * KD * T

        def a_qk(part, which, hh):
            at = A_2 + ((part * 2 + which) * 2 + hh) * T
            return arena[:, at:at + T]

        def a_dv(part, hh, t, rows=P, nt=1):
            at = A_2 + 8 * T + ((part * 2 + hh) * 5 + t) * P
            return arena[0:rows, at:at + nt * P]

        def a_dpt(part, slot, t, rows=P, nt=1):
            at = A_2 + 8 * T + 20 * P + ((part * 2 + slot) * 6 + 1 + t) * P
            return arena[0:rows, at:at + nt * P]

        def a_hid(part, k):
            at = (part * KD + k) * T
            return arena[:, at:at + T]

        def so(hh):
            return acc[:, hh * S:hh * S + S]
        AX = [acc[:, 2048:2560], acc[:, 2560:3072]]
        G0, G1 = acc[:, 3072:3584], acc[:, 3584:4096]

        raw_in = [sem("raw_in0"), sem("raw_in1")]
        whi, wlo = sem("whi"), sem("wlo")
        ps_full, ps_free = sem("ps_full"), sem("ps_free")
        h_in = [sem(f"h_in{k}") for k in range(KD)]
        small_in, pos_in, meta_in, p_in = sem("small_in"), sem("pos_in"), sem("meta_in"), sem("p_in")
        lam_in = sem("lam_in")
        out_sem = sem("out_sem")
        zhi, zlo = sem("zhi"), sem("zlo")
        squared, summed, stat, rooted, rstd = sem("squared"), sem("summed"), sem("stat"), sem("rooted"), sem("rstd")
        scaled, resid = sem("scaled"), sem("resid")
        acc_zero = sem("acc_zero")
        consts = sem("consts")
        names = {}

        def s(name):
            if name not in names:
                names[name] = sem(name)
            return names[name]

        def wait(eng, semaphore, n):
            eng.wait_ge(semaphore, n)

        def banks(slot, o, ntok, rows=P):
            b = 4 * slot + 2 * o
            return ps[0:rows, b, 0:ntok] if ntok <= 512 else ps[0:rows, b:b + 2, 0:HALF]

        def like(ap, ntok):
            return ap if ntok <= 512 else ap.rearrange("p (a b) -> p a b", a=2)

        block = ctx.enter_context(nc.Block())

        @block.sync
        def _(sp):
            sp.dma_start(so(1).bitcast(i32), pos).then_inc(pos_in, 16)
            sp.dma_start(sm[:, :], small).then_inc(small_in, 16)
            sp.dma_start(w_raw[:, 0, :], wstream[0]).then_inc(raw_in[0], 16)
            for k in range(KD):
                sp.dma_start(h[:, k, META:T], xT[k]).then_inc(h_in[k], 16)
            sp.dma_start(w_raw[:, 1, :], wstream[1]).then_inc(raw_in[1], 16)
            sp.dma_start(h[:, :, 0:META], metaT).then_inc(meta_in, 16)
            sp.dma_start(acc[:, 0:256], lam).then_inc(lam_in, 16)
            with sp.Fori(1, B_MLP1 // 2) as i:
                for j in range(2):
                    sp.wait_ge(wlo, 2 * i + (j - 1))
                    sp.dma_start(w_raw[:, j, :], wstream[2 * i + j]).then_inc(raw_in[j], 16)
            sp.wait_ge(s("qr_lo"), 2)
            sp.dma_start(rope_cs[:, :, :].rearrange("p a b -> p (a b)"), pT).then_inc(p_in, 16)
            with sp.Fori(B_MLP1 // 2, NBLK // 2) as i:
                for j in range(2):
                    sp.wait_ge(wlo, 2 * i + (j - 1))
                    sp.dma_start(w_raw[:, j, :], wstream[2 * i + j]).then_inc(raw_in[j], 16)
            for k in range(KD):
                sp.wait_ge(resid, 8 * 5 + k + 1)
                sp.dma_start(out[k], h[:, k, META:T]).then_inc(out_sem, 16)
            sp.wait_ge(out_sem, 16 * KD)

        def act_hi(act, slot, n_raw, n_full):
            act.wait_ge(raw_in[slot], 16 * n_raw)
            if n_full is not None:
                act.wait_ge(ps_full, n_full)
            act.activation(w_hi[:, slot, :], w_raw[:, slot, :], ACT.Copy).then_inc(whi, 1)

        def used(i):
            return 2 * pair_of(i + 1)

        def act_next(act, i):
            act_hi(act, i % 2, i // 2 + 1, used(i - 2) if i >= 2 else None)

        def dve_lo(dve, i, slot):
            dve.wait_ge(whi, i + 1)
            dve.tensor_tensor(w_lo[:, slot, :], w_raw[:, slot, :], w_hi[:, slot, :].bitcast(f32),
                              ALU.subtract).then_inc(wlo, 1)

        def project(pe, wslot, slot, first_tile, nk, z, ntok, before, z_ready=None):
            if before is not None:
                pe.wait_ge(ps_free, before)
            cuts = [(0, ntok)] if ntok <= 512 else [(0, HALF), (HALF, T)]
            for k in range(nk):
                if z_ready is not None:
                    z_ready(k)
                for o in range(2):
                    at = ((first_tile + o) * nk + k) * P
                    wh, wl = w_hi[:, wslot, at:at + P], w_lo[:, wslot, at:at + P]
                    for c, (a, b) in enumerate(cuts):
                        dst = ps[:, 4 * slot + 2 * o + c, 0:b - a]
                        zh, zl = z(0, k)[:, a:b], z(1, k)[:, a:b]
                        pe.matmul(dst, wh, zh, start=(k == 0), stop=False)
                        pe.matmul(dst, wh, zl, start=False, stop=False)
                        last = pe.matmul(dst, wl, zh, start=False, stop=(k == nk - 1))
                    if k == nk - 1:
                        last.then_inc(ps_full, 1)

        def z_part(part, k):
            return (z_hi if part == 0 else z_lo)[:, k, :]

        def pe_stat(pe, si, slot, ntok, c0):
            pe.wait_ge(summed, 8 * (si + 1))
            if ntok <= 512:
                pe.matmul(ps[:, 4 * slot, 0:ntok], ones[:, :], ssum[:, c0:c0 + ntok], start=True, stop=True).then_inc(stat, 1)
            else:
                for c in range(2):
                    last = pe.matmul(ps[:, 4 * slot + c, 0:HALF], ones[:, :], ssum[:, c * HALF:(c + 1) * HALF], start=True, stop=True)
                last.then_inc(stat, 1)

        def starts(ntok):
            return [P * i for i in range(4)] if ntok <= 512 else [b + a for b in (0, HALF) for a in (0, P, HALF - P)]

        R_COL = 105

        def pe_columns(pe, dst, srcs, ntok):
            for i, a in enumerate(starts(ntok)):
                for k, src in enumerate(srcs):
                    last = pe.matmul(dst[:, i:i + 1], src[:, a:a + P], ones[:, 0:1], start=(k == 0), stop=(k == len(srcs) - 1))
            return last

        def pe_spread(pe, bank, src, ntok):
            for i, a in enumerate(starts(ntok)):
                dst = ps[:, bank, a:a + P] if ntok <= 512 else ps[:, bank + a // HALF, a % HALF:a % HALF + P]
                last = pe.matmul(dst, src[:, i:i + 1].to_broadcast([P, P]), ident[:, :], start=True, stop=True)
            return last

        def pe_post_stat(pe, pi, ntok, c0):
            si, (bank, col_bank) = 2 * pi + 1, post_banks(pi, ntok)
            pe.wait_ge(summed, 8 * (si + 1))
            pe_columns(pe, ps[:, col_bank, :], [ssum[:, c0:c0 + ntok]], ntok).then_inc(stat, 1)
            pe.wait_ge(rstd, si + 1)
            pe_spread(pe, bank, cols[:, R_COL:R_COL + 6], ntok).then_inc(s("spread"), 1)

        def act_load(act, func):
            act.activation(cols[:, 119:120], eps[:, 1:2], func).then_inc(s("loaded"), 1)

        def act_root(act, si, slot, ntok, c0):
            act.wait_ge(stat, si + 1)
            dst = rr[:, si % 2, c0:c0 + ntok]
            act.activation(like(dst, ntok), banks(slot, 0, ntok), ACT.Sqrt, bias=eps[:, 0:1], scale=1.0 / D).then_inc(rooted, 1)

        def dve_rstd(dve, si, ntok, c0):
            dve.wait_ge(rooted, si + 1)
            dst = rr[:, si % 2, c0:c0 + ntok]
            dve.reciprocal(dst, dst).then_inc(rstd, 1)

        def act_square(act, si, k, src, ntok, c0):
            if 8 * si + k >= 2:
                act.wait_ge(summed, 8 * si + k - 1)
            act.activation(sq[:, k % 2, c0:c0 + ntok], src, ACT.Square).then_inc(squared, 1)

        def pool_sum(pool, si, ntok, c0):
            for k in range(KD):
                pool.wait_ge(squared, 8 * si + k + 1)
                if k == 0:
                    if si:
                        pool.wait_ge(stat, si)
                    pool.tensor_copy(ssum[:, c0:c0 + ntok], sq[:, 0, c0:c0 + ntok]).then_inc(summed, 1)
                else:
                    pool.wait_ge(summed, 8 * si + k)
                    pool.tensor_tensor(ssum[:, c0:c0 + ntok], ssum[:, c0:c0 + ntok], sq[:, k % 2, c0:c0 + ntok],
                                       ALU.add).then_inc(summed, 1)

        GAIN = {0: ("attn_pre", 0), 1: ("ffn_pre", 0), 3: ("norm2", 0), 4: ("norm2", 16), 5: ("norm2", 32), 6: ("norm2", 48)}

        def act_zhi(act, zi, k, c0):
            g = 1.0 if zi == 2 else smc(GAIN[zi][0], GAIN[zi][1] + k)
            act.activation(z_hi[:, k, 0:T - c0], h[:, k, c0:T], ACT.Copy, scale=g).then_inc(zhi, 1)

        def dve_zlo(dve, zi, k, c0):
            dve.wait_ge(zhi, 8 * zi + k + 1)
            hk, zk = h[:, k, c0:T], z_hi[:, k, 0:T - c0].bitcast(f32)
            if zi == 2:
                dve.tensor_tensor(z_lo[:, k, 0:T - c0], hk, zk, ALU.subtract).then_inc(zlo, 1)
            else:
                dve.scalar_tensor_tensor(z_lo[:, k, 0:T - c0], hk, smc(GAIN[zi][0], GAIN[zi][1] + k), zk,
                                         op0=ALU.mult, op1=ALU.subtract).then_inc(zlo, 1)

        POST = {0: ("attn_post", 0), 1: ("ffn_post", 0), 2: ("norm2", 8), 3: ("norm2", 24), 4: ("norm2", 40), 5: ("norm2", 56)}
        NEXT_Z = {0: 1, 1: 2, 2: 4, 3: 5, 4: 6}

        def act_post(act, pi, p_out, ntok, c0, nxt_c0=None, between=None):
            si = 2 * pi + 1
            for k in range(KD):
                if k == KD - 1:
                    act_load(act, ACT.Sqrt)
                act.wait_ge(ps_free, 2 * p_out + k + 1)
                act_square(act, si, k, ac(k)[:, c0:T], ntok, c0)
            if between:
                between()
            act.wait_ge(stat, si + 1)
            n = len(starts(ntok))
            act.activation(cols[:, R_COL:R_COL + n], ps[:, post_banks(pi, ntok)[1], 0:n], ACT.Sqrt, bias=eps[:, 0:1],
                           scale=1.0 / D).then_inc(rooted, 1)
            if pi == 5:
                return
            zi = NEXT_Z[pi]
            for k in range(KD):
                act.wait_ge(resid, 8 * pi + k + 1)
                if k == 0:
                    act.wait_ge(ps_full, 2 * p_out + 8)
                act_zhi(act, zi, k, nxt_c0)
                if zi != 2:
                    act_square(act, si + 1, k, h[:, k, c0:T], ntok, c0)

        def dve_post(dve, pi, ntok, c0, nxt_c0=None, between=None):
            si = 2 * pi + 1
            n = len(starts(ntok))
            bank = post_banks(pi, ntok)[0]
            roots = ps[:, bank, 0:S] if ntok <= 512 else ps[:, bank:bank + 2, 0:HALF]
            dve.wait_ge(rooted, si + 1)
            dve.reciprocal(cols[:, R_COL:R_COL + n], cols[:, R_COL:R_COL + n]).then_inc(rstd, 1)
            dve.wait_ge(s("spread"), pi + 1)
            for k in range(KD + 1):
                if k < KD:
                    t = like(ac(k)[:, c0:T], ntok)
                    dve.scalar_tensor_tensor(t, t, smc(POST[pi][0], POST[pi][1] + k), roots,
                                             op0=ALU.mult, op1=ALU.mult).then_inc(scaled, 1)
                    dve.wait_ge(scaled, 8 * pi + k + 1)
                    dve.tensor_tensor(h[:, k, c0:T], h[:, k, c0:T], ac(k)[:, c0:T], ALU.add).then_inc(resid, 1)
                if k and pi != 5:
                    dve_zlo(dve, NEXT_Z[pi], k - 1, nxt_c0)
                if between and k == 2:
                    between()

        def z_ready_for(pe, zi):
            return lambda k: pe.wait_ge(zlo, 8 * zi + k + 1)


        def dve_take(dve, p, o, ntok, dst, r=None, then=None):
            dve.wait_ge(ps_full, 2 * p + o + 1)
            src = banks(p % 2, o, ntok)
            if r is None:
                dve.tensor_copy(like(dst, ntok), src).then_inc(ps_free, 1)
            else:
                dve.tensor_tensor(like(dst, ntok), src, like(r, ntok), ALU.mult).then_inc(ps_free, 1)

        def once(dve, name, n, ins):
            ins.then_inc(s(name), 1)
            dve.wait_ge(s(name), n)

        P_IN, P_UQ, P_UKV, P_OUT1, P_MLP1, P_PLEP, P_PLEG, P_QKV, P_OUT2, P_MLP2, P_CONV, P_OUT3, P_MLP3 = (
            pair_of(b) for b in (B_IN, B_UQ, B_UKV, B_OUT1, B_MLP1, B_PLEP, B_PLEG, B_QKV, B_OUT2, B_MLP2,
                                 B_CONV, B_OUT3, B_MLP3))
        def post_banks(pi, ntok):
            if ntok <= 512:
                return 1, 3
            slot = ({2: P_MLP2, 3: P_CONV}[pi] + 1) % 2
            return 4 * slot, 4 * slot + 2
        def c_square(k):
            return (rr[:, 1, 0:S], sq[:, 0, 0:S], sq[:, 1, 0:S])[k]
        RX = rr[:, 0, META:T]
        SC1 = QKD ** -0.5
        SC2 = (D // (2 * DIFF_HEADS)) ** -0.5
        SCM = P ** -0.5
        UG = 10

        def unit(u, c):
            b = u % 5
            nq, nk = (META, META) if b == 0 else (P, META + P * b)
            return nq, nk, tt(u % UG % 3 * 2 + c, nk, nq)

        D_MAX, D_NMX, D_SUM, D_RC = 0, 6, 12, 18

        def s_cut(u, c):
            nq, nk, _ = unit(u, c)
            b = s_bank(u) + 2 * c
            return ps[0:nq, b:b + 2, 0:HALF] if nk > 512 else ps[0:nq, b + u % 5 % 2, 0:nk]

        def s_bank(u):
            return 4 * ((P_QKV + 3 * (u // UG) + 1) % 2)

        def t_bank(u):
            return 4 - s_bank(u)

        def d_parts(u):
            return 2 * (u + 1) - (u // 5 + 1)

        @block.gpsimd
        def _(pool):
            pool.memset(ident[:, :], 0.0).then_inc(consts, 1)
            pool.memset(tri[:, :], 0.0).then_inc(consts, 1)
            pool.memset(dist[:, :], 0.0).then_inc(consts, 1)
            pool.memset(eps[:, 0:1], EPS).then_inc(consts, 1)
            pool.memset(eps[:, 1:2], 1.0).then_inc(consts, 1)
            pool.memset(eps[:, 2:3], EPS / (1 - LAM_INIT) ** 2).then_inc(consts, 1)
            pool.memset(eps[:, 3:4], 0.0).then_inc(consts, 1)
            pool.memset(ones[:, :], 1.0).then_inc(consts, 1)
            pool.memset(ones_r[:, :].bitcast(f32), 1.0).then_inc(consts, 1)
            for part in range(2):
                pool.wait_ge(consts, 9 + 2 * part)
                pool.memset(a_kpe(part, 0, 64, P).bitcast(f32), 0.0).then_inc(consts, 1)
                pool.wait_ge(consts, 10 + 2 * part)
                pool.memset(a_kpe(part, 1, 0, 64).bitcast(f32), 0.0).then_inc(consts, 1)
            pool.wait_ge(consts, 13)
            pool.affine_select(out=ident[:, :], in_=ident[:, :], compare_op=ALU.not_equal, fill=1.0, base=0,
                               pattern=[[-1, P]], channel_multiplier=1).then_inc(consts, 1)
            pool.affine_select(out=tri[:, :], in_=tri[:, :], compare_op=ALU.is_ge, fill=NEG, base=0,
                               pattern=[[1, P]], channel_multiplier=-1).then_inc(consts, 1)
            pool.affine_select(out=dist[:, 0:S], in_=dist[:, 0:S], compare_op=ALU.is_ge, fill=NEG, base=S - P,
                               pattern=[[-1, S]], channel_multiplier=1).then_inc(consts, 1)
            pool_sum(pool, 0, S, META)
            pool.wait_ge(stat, 1)
            sel = ssum[0:4, 0:S].rearrange("p (a b) -> p a b", a=4)
            pool.memset(ssum[0:4, 0:S], 0.0).then_inc(s("sel"), 1)
            pool.wait_ge(s("sel"), 1)
            pool.affine_select(out=sel, in_=sel, compare_op=ALU.not_equal, fill=1.0, base=0,
                               pattern=[[-1, 4], [0, P]], channel_multiplier=1).then_inc(s("sel"), 1)
            pool.wait_ge(s("bc"), 4)
            pool_sum(pool, 1, S, META)
            pool_sum(pool, 2, S, META)

            def zero_acc(pi):
                pool.wait_ge(resid, 8 * pi + 8)
                pool.memset(acc[:, :], 0.0).then_inc(acc_zero, 1)
            zero_acc(0)
            pool_sum(pool, 3, S, META)
            pool.wait_ge(s("a_max"), 16)
            pool.iota(dist[:, :], pattern=[[1, T]], base=-(S - P + META), channel_multiplier=-1,
                      allow_small_or_imprecise_dtypes=True).then_inc(s("dist"), 1)
            pool.wait_ge(s("dist"), 1)
            pool.affine_select(out=dist[:, :], in_=dist[:, :], compare_op=ALU.is_ge, fill=NEG, base=S - P + META,
                               pattern=[[-1, T]], channel_multiplier=1).then_inc(s("dist"), 1)
            pool_sum(pool, 4, T, 0)
            pool_sum(pool, 5, T, 0)
            pool_sum(pool, 6, T, 0)
            zero_acc(2)
            pool_sum(pool, 7, T, 0)
            pool_sum(pool, 8, T, 0)
            pool_sum(pool, 9, S, META)
            pool_sum(pool, 10, S, META)
            zero_acc(4)
            pool_sum(pool, 11, S, META)

        @block.scalar
        def _(act):
            act_next(act, 0)
            act.wait_ge(small_in, 16)
            act.wait_ge(consts, 13)
            for k in range(KD):
                act.wait_ge(h_in[k], 16)
                act_zhi(act, 0, k, META)
                act_square(act, 0, k, h[:, k, META:T], S, META)
            act_next(act, 1)
            act_root(act, 0, 1, S, META)
            act_next(act, 2)
            for k in range(3):
                act.wait_ge(ps_free, k + 1)
                if k == 0:
                    act.wait_ge(stat, 1)
                act.activation(c_square(k), so(k), ACT.Square).then_inc(s("c_sq"), 1)
            act_next(act, 3)
            act.wait_ge(s("c_stat"), 2)
            act.activation(cols[:, R_COL:R_COL + 4], ps[:, 1, 0:4], ACT.Sqrt, bias=eps[:, 0:1], scale=1.0 / 256).then_inc(s("c_root"), 1)
            act.activation(cols[:, R_COL + 4:R_COL + 8], ps[:, 5, 0:4], ACT.Sqrt, bias=eps[:, 0:1], scale=1.0 / 128).then_inc(s("c_root"), 1)
            act.wait_ge(s("angle"), 2)
            act.activation(rope_cs[:, 0, :], rope_cs[:, 0, :], ACT.Sin).then_inc(s("cs"), 1)
            act.activation(rope_cs[:, 1, :], rope_cs[:, 1, :], ACT.Sin).then_inc(s("cs"), 1)
            for j0 in range(0, 8, 2):
                act_next(act, 4 + j0 // 2)
                for q in range(2):
                    j = j0 + q
                    act.wait_ge(ps_free, 2 * 3 + j + 1)
                    act.activation(tt(2 + q, S), tt(q)[:, 4:4 + S], ACT.Identity, bias=smc("conv_b", j),
                                   scale=smc("conv_w", 24 + j)).then_inc(s("cv_y"), 1)
                for q in range(2):
                    j = j0 + q
                    act.wait_ge(s("cv_acc"), 3 * j0 + 5 + q)
                    if j >= 2:
                        act.wait_ge(s("cv_lo"), j - 1)
                    act.activation(tt(4 + q, S), tt(2 + q, S), ACT.Silu).then_inc(s("cv_s"), 1)
                for q in range(2):
                    j = j0 + q
                    act.wait_ge(s("cv_s"), j + 1)
                    act.activation(a_mqk(0, j), tt(4 + q, S), ACT.Copy).then_inc(s("cv_hi"), 1)

            def v_hi(g):
                act.wait_ge(s("v_tr"), g + 1)
                act.activation(a_v(0, g % 4), ps[:, 3 + 4 * (g % 2), :], ACT.Copy).then_inc(s("v_hi"), 1)
            act_next(act, 8)
            for k in range(3):
                act.wait_ge(s("c_norm"), k + 1)
                act.activation(a_c(0, k), so(k), ACT.Copy).then_inc(s("c_hi"), 1)
            act_next(act, 9)
            act.wait_ge(s("kr_sum"), 1)
            act.activation(a_kpe(0, 0, 0, 64), AX[0][0:64, :], ACT.Copy).then_inc(s("kr_hi"), 1)
            act.activation(a_kpe(0, 1, 64, P), AX[0][64:P, :], ACT.Copy).then_inc(s("kr_hi"), 1)
            act.wait_ge(s("lamsum"), 2)
            act.activation(cols[:, 82:84], cols[:, 80:82], ACT.Exp).then_inc(s("lamexp"), 1)
            act.wait_ge(s("g_abs"), 1)
            act.activation(AX[0][0:4, :], AX[0][0:4, :], ACT.Exp, scale=-1.0).then_inc(s("g_exp"), 1)
            act.wait_ge(s("g_exp"), 1)
            act.activation(AX[0][0:4, :], AX[0][0:4, :], ACT.Ln, bias=eps[0:4, 1:2]).then_inc(s("g_exp"), 1)
            v_hi(0)
            v_hi(1)
            act_next(act, 10)
            for hh in range(4):
                if hh == 2:
                    v_hi(2)
                    v_hi(3)
                    act_next(act, 11)
                act.wait_ge(ps_free, 2 * 9 + hh + 1)
                act.activation(so(hh), tt(4 + hh % 2, S), ACT.Sigmoid).then_inc(s("so"), 1)
            act_next(act, 12)
            def m_exps(hh):
                act.wait_ge(s("bc"), hh + 1)
                act.wait_ge(s("m_d"), 4 * hh + 4)
                if hh:
                    act.wait_ge(s("m_h"), 6 * hh - 5)
                act.activation(sq[:, 0, 0:S], ps[:, 5, :], ACT.Exp).then_inc(s("m_e"), 1)
                for kb in range(4):
                    e = tmp[:, KB_AT[kb]:KB_AT[kb] + KB_N[kb]]
                    gc = cols[:, 64 + 4 * kb + hh:65 + 4 * kb + hh]
                    act.activation(e[:, 0:P], tmp[:, 2560 + kb * P:2560 + kb * P + P], ACT.Exp, bias=gc).then_inc(s("m_e"), 1)
                    if kb < 3:
                        act.activation(e[:, P:], ps[:, 1, (kb + 1) * P:S], ACT.Exp, bias=gc).then_inc(s("m_e"), 1)
            m_exps(0)
            for hh in range(4):
                act.wait_ge(s("m_p"), 4 * hh + 4)
                act.activation(a_p(0), tmp[:, PACK:2 * PACK], ACT.Copy).then_inc(s("m_hi"), 1)
                act.wait_ge(s("m_nd"), hh + 1)
                act.activation(sq[:, 1, 0:S], ps[:, 7, :], ACT.Abs).then_inc(s("m_abs"), 1)
                if hh < 3:
                    m_exps(hh + 1)
                act.wait_ge(s("m_h"), 6 * hh + 3)
                act.activation(rr[:, 1, 0:S], rr[:, 0, 0:S], ACT.Square).then_inc(s("m_sq"), 1)
                act.wait_ge(s("m_st"), hh + 1)
                act.activation(rr[:, 1, 0:S], ps[:, 3, :], ACT.Sqrt, bias=eps[:, 0:1], scale=1.0 / P).then_inc(s("m_root"), 1)
                act.wait_ge(s("m_h"), 6 * hh + 6)
                act.activation(z_hi[:, 4 + hh, 0:S], rr[:, 0, 0:S], ACT.Copy).then_inc(s("m_zhi"), 1)
            for j in range(4):
                act.wait_ge(ps_full, 2 * P_UQ + j + 1)
                act.activation(a_q(0, j), banks((P_UQ + j // 2) % 2, j % 2, S), ACT.Copy).then_inc(s("q_hi"), 1)
            for j in range(2):
                act.wait_ge(s("qr_sum"), j + 1)
                act.activation(a_q(0, 4 + j), AX[j], ACT.Copy).then_inc(s("q_hi"), 1)
            act_next(act, 13)
            for j in range(4):
                act.wait_ge(ps_full, 2 * P_UKV + j + 1)
                act.activation(a_k(0, j), banks((P_UKV + j // 2) % 2, j % 2, S), ACT.Copy).then_inc(s("q_hi"), 1)
            for g in range(4, 8):
                v_hi(g)
            act_next(act, 14)

            def mla_exp(u):
                q = u % 4
                n = P * (u % 4 + 1)
                act.wait_ge(s("a_nmx"), u + 1)
                act.activation(tt(q, n), tt(q, n), ACT.Exp, bias=cols[:, 16 + u:17 + u], scale=SC1,
                               accum_out=cols[:, 32 + u:33 + u]).then_inc(s("a_exp"), 1)

            def mla_hi(u):
                act.wait_ge(s("a_tr"), u + 1)
                n = P * (u % 4 + 1)
                act.activation(a_pt(0, u % 2, n), ps[:, 2 + 4 * (u % 2), 0:n], ACT.Copy).then_inc(s("a_hi"), 1)

            def mla_out(u):
                act.wait_ge(s("a_pv"), u + 1)
                hh, b = divmod(u, 4)
                act.activation(z_hi[:, hh, P * b:P * b + P], ps[:, 1 + 4 * (u % 2), P:2 * P], ACT.Copy).then_inc(s("a_zhi"), 1)
            mla_exp(0)
            for u in range(16 + 2):
                if 1 <= u < 17:
                    mla_hi(u - 1)
                if u + 1 < 16:
                    mla_exp(u + 1)
                if u >= 2:
                    mla_out(u - 2)
            for j in range(2, 4):
                act_next(act, B_OUT1 + j)
            act_next(act, B_MLP1)
            act_post(act, 0, P_OUT1, S, META, nxt_c0=META)
            done = 0
            for c, nt in enumerate(CHUNKS1):
                b0, p0 = B_MLP1 + done + 4 * c, P_MLP1 + done + 4 * c
                for j in range(nt):
                    act_next(act, b0 + j + 1)
                    n = done + j
                    if n == 0:
                        act_root(act, 2, (P_MLP1 + 1) % 2, S, META)
                    q = n % 2
                    act.wait_ge(ps_free, 2 * (p0 + j) + 1)
                    act.activation(tt(2 + q, S), tt(q, S), ACT.Silu).then_inc(s("sw_silu"), 1)
                    act.wait_ge(s("sw_hm"), n + 1)
                    act.wait_ge(ps_full, 2 * p0)
                    act.activation(a_hid(0, j)[:, 0:S], tt(4 + q, S), ACT.Copy).then_inc(s("sw_hi"), 1)
                if c == len(CHUNKS1) - 1:
                    act.wait_ge(p_in, 16)
                    for k in range(2):
                        act.activation(a_ple(0, k), rope_cs[:, k, :], ACT.Copy).then_inc(s("p_hi"), 1)
                for j in range(4):
                    act_next(act, b0 + nt + j + 1)
                done += nt
            p_out1 = P_PLEP - 4
            act_post(act, 1, p_out1, S, META, nxt_c0=META, between=lambda: act_next(act, B_PLEG))
            for k in range(KD):
                if k % 2 == 0:
                    act_next(act, B_PLEG + k // 2 + 1)
                act.wait_ge(ps_full, 2 * P_PLEG + k + 1)
                if k >= 2:
                    act.wait_ge(ps_free, 2 * P_PLEG + k - 1)
                act.activation(tt(2 + k % 2, S), banks((P_PLEG + k // 2) % 2, k % 2, S), ACT.Sigmoid).then_inc(s("ple_s"), 1)
            act.wait_ge(meta_in, 16)
            for k in range(KD):
                act.wait_ge(s("ple_h"), k + 1)
                act_zhi(act, 3, k, 0)
                act_square(act, 4, k, h[:, k, :], T, 0)

            def d_exp(u):
                for c in range(2):
                    act.wait_ge(s("d_nmx"), 2 * u + c + 1)
                    nq, nk, t = unit(u, c)
                    w = u % UG % 3 * 2 + c
                    act.activation(t, t, ACT.Exp, bias=cols[0:nq, D_NMX + w:D_NMX + w + 1], scale=SC2,
                                   accum_out=cols[0:nq, D_SUM + w:D_SUM + w + 1]).then_inc(s("d_exp"), 1)

            def d_hi(u):
                nq, nk, _ = unit(u, 0)
                act.wait_ge(s("d_tr"), u + 1)
                act.activation(a_dpt(0, u % 2, 0, META)[:, 0:nq], ps[0:META, t_bank(u) + 2 + u % 2, 0:nq], ACT.Copy).then_inc(s("d_hi"), 1)
                if nk > META:
                    act.activation(a_dpt(0, u % 2, 1, P, (nk - META) // P), ps[:, t_bank(u) + u % 2, 0:nk - META], ACT.Copy).then_inc(s("d_hi"), 1)

            def sub_squares(g):
                act.wait_ge(s("d_o"), UG * (g + 1))
                for i in range(2):
                    act.activation(sq[:, i, :], ac(2 * g + i), ACT.Square).then_inc(s("d_sq"), 1)

            def sub_roots(g, base):
                for i in range(2):
                    act.wait_ge(s("d_st"), 2 * g + i + 1)
                    act.activation(like(sq[:, i, :], T), ps[:, base + 2 * i:base + 2 * i + 2, 0:HALF], ACT.Sqrt,
                                   bias=eps[:, 2:3], scale=1.0 / (P * (1 - LAM_INIT) ** 2)).then_inc(s("d_root"), 1)

            def sub_high(g):
                for i in range(2):
                    act.wait_ge(s("d_n"), 4 * g + 2 + i + 1)
                    act.activation(a_out(0, 2 * g + i), ac(2 * g + i), ACT.Copy).then_inc(s("d_ohi"), 1)

            for g in range(GROUPS):
                b0, p0 = B_QKV + 3 * g, P_QKV + 3 * g
                for i in range(2):
                    act_next(act, b0 + i + 1)
                    if g == 0 and i == 0:
                        act_root(act, 4, (P_QKV + 1) % 2, T, 0)
                    if g and i == 0:
                        sub_squares(g - 1)
                    for o in range(2):
                        act.wait_ge(ps_free, 2 * (p0 + i) + o + 1)
                        act.activation(a_qk(0, o, i), tt(2 * i + o), ACT.Copy).then_inc(s("dq_hi"), 1)
                    if g and i == 0:
                        sub_roots(g - 1, 4 * ((p0 + 1) % 2))
                        sub_high(g - 1)
                act_next(act, b0 + 3)
                act_load(act, ACT.Exp)
                tb = t_bank(UG * g)
                for i in range(2):
                    act.wait_ge(s("dv_tr"), 2 * g + i + 1)
                    act.activation(a_dv(0, i, 1, P, 4), ps[:, tb + i, :], ACT.Copy).then_inc(s("dv_hi"), 1)
                    act.activation(a_dv(0, i, 0, META), ps[0:META, tb + 2 + i, 0:P], ACT.Copy).then_inc(s("dv_hi"), 1)
                first = UG * g
                d_exp(first)
                for u in range(first, first + UG + 1):
                    if u >= first + 1:
                        d_hi(u - 1)
                    if u + 1 < first + UG:
                        d_exp(u + 1)
            sub_squares(GROUPS - 1)
            sub_roots(GROUPS - 1, 0)
            sub_high(GROUPS - 1)
            for j in range(1, 4):
                act_next(act, B_OUT2 + j)
            act_next(act, B_MLP2)
            act_post(act, 2, P_OUT2, T, 0, nxt_c0=0)

            def act_mlp(l, b0, p0, si, ntok):
                def chunk(c, last=False):
                    head = isinstance(c, int) and c == 0
                    for j in range(KD // 2):
                        act_hi(act, (b0 + j + 1) % 2, (b0 + j + 1) // 2 + 1 + 4 * c, 2 * (p0 + j) + 16 * c)
                        if head and j == 0:
                            act_root(act, si, (p0 + 1) % 2, ntok, T - ntok)
                        for o in range(2):
                            n = FF2 * l + 2 * j + o + 8 * c
                            act.wait_ge(ps_free, 2 * (p0 + j) + o + 1 + 16 * c)
                            if not (head and n < 2):
                                act.wait_ge(s("hid_lo"), n - 1)
                            act.activation(tt(2 + o, ntok), tt(o, ntok), ACT.Square).then_inc(s("hid_a"), 1)
                        for o in range(2):
                            n = FF2 * l + 2 * j + o + 8 * c
                            act.wait_ge(s("hid_a"), n + 1)
                            act.activation(a_hid(0, 2 * j + o)[:, 0:ntok], tt(2 + o, ntok), ACT.Copy).then_inc(s("hid_hi"), 1)
                    for j in range(4, 8):
                        if not (last and j == 7):
                            act_hi(act, (b0 + j + 1) % 2, (b0 + j + 1) // 2 + 1 + 4 * c, 2 * (p0 + j) + 16 * c)
                return chunk
            mlp = act_mlp(0, B_MLP2, P_MLP2, 6, T)
            mlp(0)
            with act.Fori(1, NCH2) as c:
                mlp(c)
            act_post(act, 3, P_CONV - 4, T, 0, nxt_c0=0)
            for m in range(4):
                p0 = P_CONV + 3 * m
                for i in range(2):
                    act_next(act, B_CONV + 3 * m + i + 1)
                    if m == 0 and i == 0:
                        act_root(act, 8, (P_CONV + 1) % 2, T, 0)
                    j = 2 * m + i
                    act.wait_ge(s("sc_v"), j + 1)
                    act.activation(tt(4 + i, S), tt(2 + i)[:, META:T], ACT.Copy, scale=smc("conv2_w", 16 + j)).then_inc(s("sc_y"), 1)
                act_next(act, B_CONV + 3 * m + 3)
                for i in range(2):
                    j = 2 * m + i
                    act.wait_ge(s("sc_o"), j + 1)
                    act.activation(a_out(0, j, 0, S), tt(i, S), ACT.Copy).then_inc(s("sc_hi"), 1)
            for j in range(1, 4):
                act_next(act, B_OUT3 + j)
            act_next(act, B_MLP3)
            act_post(act, 4, P_OUT3, S, META, nxt_c0=META)
            mlp = act_mlp(1, B_MLP3, P_MLP3, 10, S)
            mlp(0)
            with act.Fori(1, NCH2 - 1) as c:
                mlp(c)
            mlp(NCH2 - 1, last=True)
            act_post(act, 5, P_MLP3 + 8 * NCH2 - 4, S, META)

        @block.vector
        def _(dve):
            dve.wait_ge(small_in, 16)
            dve.wait_ge(pos_in, 16)
            n_ang = 0

            def ang(ins):
                nonlocal n_ang
                n_ang += 1
                once(dve, "ang", n_ang, ins)
            MAGIC = 1.5 * 2.0 ** 23
            C1 = 6.28125
            C2 = float(np.float32(np.floor((2 * math.pi - C1) * 2.0 ** 21) / 2.0 ** 21))
            C3 = 2 * math.pi - C1 - C2
            PI32 = 3.1415925
            ang(dve.tensor_copy(so(2), so(1).bitcast(i32)))

            def angles(w):
                name, off = [("freq", 0.25), ("sfreq", 0.0)][w]
                r = rope_cs[:, w, :]
                ang(dve.tensor_scalar(r, so(2), smc(name), None, ALU.mult))
                ang(dve.tensor_scalar(so(3), r, 1 / (2 * math.pi), off, ALU.mult, ALU.add))
                ang(dve.tensor_scalar(so(3), so(3), MAGIC, None, ALU.add))
                ang(dve.tensor_scalar(so(3), so(3), MAGIC, None, ALU.subtract))
                for cc in (C1, C2, C3):
                    ang(dve.scalar_tensor_tensor(r, so(3), -cc, r, op0=ALU.mult, op1=ALU.add))
                ang(dve.tensor_scalar(r, r, 2 * math.pi * off, PI32, ALU.add, ALU.min))
                dve.tensor_scalar(r, r, -PI32, None, ALU.max).then_inc(s("angle"), 1)
            angles(0)
            dve_lo(dve, 0, 0)
            for k in range(KD):
                dve_zlo(dve, 0, k, META)
            dve_lo(dve, 1, 1)
            angles(1)
            dve.wait_ge(lam_in, 16)
            for w in range(2):
                dve.tensor_tensor_reduce(out=so(3)[:, 64 * w:64 * w + 64], in0=acc[:, 128 * w:128 * w + 64],
                                         in1=acc[:, 128 * w + 64:128 * w + 128], scale=1.0, scalar=0.0,
                                         op0=ALU.mult, op1=ALU.add, accum_out=cols[:, 80 + w:81 + w]).then_inc(s("lamsum"), 1)
            dve.wait_ge(s("lamsum"), 2)
            dve_rstd(dve, 0, S, META)
            dve.wait_ge(rstd, 1)
            for o in range(2):
                dve_take(dve, 0, o, S, so(o), RX)
            dve_lo(dve, 2, 0)
            dve_take(dve, 1, 0, S, so(2), RX)
            dve.wait_ge(ps_full, 4)
            dve.tensor_tensor(G0[0:4, :], ps[0:4, 6, :], RX[0:4, :], ALU.mult).then_inc(s("gate"), 1)
            dve.tensor_tensor(G1[32:36, :], ps[32:36, 6, :], RX[32:36, :], ALU.mult).then_inc(ps_free, 1)
            dve_lo(dve, 3, 1)
            for o in range(2):
                dve_take(dve, 2, o, S, AX[o], RX)
            dve.wait_ge(s("c_root"), 2)
            dve.reciprocal(cols[:, R_COL:R_COL + 8], cols[:, R_COL:R_COL + 8]).then_inc(s("c_rcp"), 1)
            dve.memset(tt(0)[:, 0:4], 0.0).then_inc(s("pad"), 1)
            dve.memset(tt(1)[:, 0:4], 0.0).then_inc(s("pad"), 1)
            dve.wait_ge(s("pad"), 2)
            for j0 in range(0, 8, 2):
                for q in range(2):
                    dve_take(dve, 3 + j0 // 2, q, S, tt(q)[:, 4:4 + S], RX)
                dve_lo(dve, 4 + j0 // 2, (j0 // 2) % 2)
                for t in range(3):
                    for q in range(2):
                        dve.wait_ge(s("cv_y"), j0 + q + 1)
                        if t:
                            dve.wait_ge(s("cv_acc"), 3 * j0 + 2 * t + q - 1)
                        dve.scalar_tensor_tensor(tt(2 + q, S), tt(q)[:, 1 + t:1 + t + S], smc("conv_w", 8 * t + j0 + q),
                                                 tt(2 + q, S), op0=ALU.mult, op1=ALU.add).then_inc(s("cv_acc"), 1)
                for q in range(2):
                    dve.wait_ge(s("cv_hi"), j0 + q + 1)
                    dve.tensor_tensor(a_mqk(1, j0 + q), tt(4 + q, S), a_mqk(0, j0 + q).bitcast(f32),
                                      ALU.subtract).then_inc(s("cv_lo"), 1)

            def v_lo(g):
                dve.wait_ge(s("v_hi"), g + 1)
                dve.tensor_tensor(a_v(1, g % 4), ps[:, 3 + 4 * (g % 2), :], a_v(0, g % 4).bitcast(f32),
                                  ALU.subtract).then_inc(s("v_lo"), 1)
            dve_lo(dve, 8, 0)
            dve.wait_ge(s("c_spread"), 2)
            for k in range(3):
                g = smc("q_norm", k) if k < 2 else smc("kv_norm")
                dve.scalar_tensor_tensor(so(k), so(k), g, ps[:, 3 if k < 2 else 7, :], op0=ALU.mult,
                                         op1=ALU.mult).then_inc(s("c_norm"), 1)
            dve.wait_ge(s("cv_s"), 8)
            for hh in range(2):
                dve_take(dve, 7, hh, S, tt(hh, S), RX)
            dve.wait_ge(s("cs"), 2)
            once(dve, "kr", 1, dve.tensor_tensor(AX[0], AX[0], rope_cs[:, 0, :], ALU.mult))
            once(dve, "kr", 2, dve.tensor_tensor(AX[1], AX[1], rope_cs[:, 1, :], ALU.mult))
            dve.tensor_tensor(AX[0], AX[0], AX[1], ALU.add).then_inc(s("kr_sum"), 1)
            for k in range(3):
                dve.wait_ge(s("c_hi"), k + 1)
                dve.tensor_tensor(a_c(1, k), so(k), a_c(0, k).bitcast(f32), ALU.subtract).then_inc(s("c_lo"), 1)
            dve_lo(dve, 9, 1)
            dve.wait_ge(s("kr_hi"), 2)
            dve.wait_ge(s("kr_sum"), 1)
            for odd, (r0, r1) in enumerate([(0, 64), (64, P)]):
                dve.tensor_tensor(a_kpe(1, odd, r0, r1), AX[0][r0:r1, :], a_kpe(0, odd, r0, r1).bitcast(f32),
                                  ALU.subtract).then_inc(s("kr_lo"), 1)
            dve.wait_ge(s("kr_lo"), 2)
            g0, g1, x0, x1 = G0[0:4, :], G1[0:4, :], AX[0][0:4, :], AX[1][0:4, :]
            once(dve, "g", 1, dve.tensor_copy(g1, G1[32:36, :]))
            once(dve, "g", 2, dve.tensor_scalar(g0, g0, smc("gate_i", rows=4), None, ALU.add))
            once(dve, "g", 3, dve.tensor_scalar(g1, g1, smc("gate_f", rows=4), None, ALU.add))
            dve.scalar_tensor_tensor(x0, g1, -1.0, g1, op0=ALU.mult, op1=ALU.max).then_inc(s("g_abs"), 1)
            once(dve, "g", 4, dve.memset(x1, 0.0))
            for hh in range(2):
                dve_take(dve, 8, hh, S, tt(2 + hh, S), RX)
            v_lo(0)
            v_lo(1)
            dve_lo(dve, 10, 0)
            dve.wait_ge(s("lamexp"), 1)
            dve.tensor_scalar(cols[:, 84:85], cols[:, 83:84], cols[:, 82:83], LAM_INIT, ALU.subtract,
                              ALU.subtract).then_inc(s("lam"), 1)
            dve.wait_ge(s("g_exp"), 2)
            once(dve, "g", 5, dve.scalar_tensor_tensor(g1, g1, 0.0, x0, op0=ALU.min, op1=ALU.subtract))
            once(dve, "g", 6, dve.tensor_copy(x0, x1))
            once(dve, "g", 7, dve.tensor_tensor_scan(out=x1, data0=g1, data1=x0, initial=0.0, op0=ALU.add, op1=ALU.add))
            once(dve, "g", 8, dve.tensor_tensor(g0, g0, x1, ALU.subtract))
            once(dve, "g", 9, dve.tensor_tensor_scan(out=g1, data0=g0, data1=x0, initial=0.0, op0=ALU.max, op1=ALU.max))
            once(dve, "g", 10, dve.tensor_scalar(x0, g1, -1.0, None, ALU.mult))
            once(dve, "g", 11, dve.scalar_tensor_tensor(x1, x1, -1.0, g1, op0=ALU.mult, op1=ALU.subtract))
            for hh in range(4):
                if hh == 2:
                    v_lo(2)
                    v_lo(3)
                    dve_lo(dve, 11, 1)
                if hh >= 2:
                    dve.wait_ge(s("so"), hh - 1)
                dve_take(dve, 9 + hh // 2, hh % 2, S, tt(4 + hh % 2, S), RX)
            dve_lo(dve, 12, 0)
            dve.wait_ge(s("so"), 4)
            dve.wait_ge(s("g_tr"), 1)
            once(dve, "gc", 1, dve.tensor_copy(cols[:, 64:80], ps[:, 1, 0:16]))

            def m_diag(hh):
                dve.wait_ge(s("bc"), hh + 1)
                if hh:
                    dve.wait_ge(s("m_e"), 8 * hh)
                for kb in range(4):
                    dve.tensor_tensor(tmp[:, 2560 + kb * P:2560 + kb * P + P], ps[:, 1, kb * P:kb * P + P],
                                      tri[:, :], ALU.add).then_inc(s("m_d"), 1)
            m_diag(0)
            for hh in range(4):
                dve.wait_ge(s("m_e"), 8 * hh + 8)
                dve.wait_ge(s("m_s"), hh + 1)
                for kb in range(4):
                    b, at = [(0, 0), (2, 0), (4, 0), (2, KB_N[1])][kb]
                    e, p = KB_AT[kb], PACK + KB_AT[kb]
                    dve.scalar_tensor_tensor(tmp[:, p:p + KB_N[kb]], ps[:, b, at:at + KB_N[kb]], SCM,
                                             tmp[:, e:e + KB_N[kb]], op0=ALU.mult, op1=ALU.mult).then_inc(s("m_p"), 1)
                dve.wait_ge(s("m_hi"), hh + 1)
                dve.tensor_tensor(a_p(1), tmp[:, PACK:2 * PACK], a_p(0).bitcast(f32), ALU.subtract).then_inc(s("m_lo"), 1)
                if hh < 3:
                    m_diag(hh + 1)
                dve.wait_ge(s("m_abs"), hh + 1)
                hs, rt = rr[:, 0, 0:S], rr[:, 1, 0:S]
                n = 6 * hh
                once(dve, "m_h", n + 1, dve.tensor_tensor(sq[:, 1, 0:S], sq[:, 1, 0:S], sq[:, 0, 0:S], ALU.max))
                once(dve, "m_h", n + 2, dve.reciprocal(sq[:, 1, 0:S], sq[:, 1, 0:S]))
                once(dve, "m_h", n + 3, dve.tensor_tensor(hs, ps[:, 6, :], sq[:, 1, 0:S], ALU.mult))
                dve.wait_ge(s("m_root"), hh + 1)
                once(dve, "m_h", n + 4, dve.reciprocal(rt, rt))
                once(dve, "m_h", n + 5, dve.scalar_tensor_tensor(hs, hs, smc("mlstm_norm", hh), rt, op0=ALU.mult, op1=ALU.mult))
                once(dve, "m_h", n + 6, dve.tensor_tensor(hs, hs, so(hh), ALU.mult))
                dve.wait_ge(s("m_zhi"), hh + 1)
                dve.tensor_tensor(z_lo[:, 4 + hh, 0:S], hs, z_hi[:, 4 + hh, 0:S].bitcast(f32), ALU.subtract).then_inc(s("m_zlo"), 1)
            def low(j, n, p, o, lo, hi):
                dve.wait_ge(s("q_hi"), n)
                dve.tensor_tensor(lo, banks(p % 2, o, S), hi.bitcast(f32), ALU.subtract).then_inc(ps_free, 1)
            for j in range(4):
                low(j, j + 1, P_UQ + j // 2, j % 2, a_q(1, j), a_q(0, j))
            for o in range(2):
                dve_take(dve, P_UQ + 2, o, S, AX[o], rope_cs[:, 0, :])
            for o in range(2):
                dve_take(dve, P_UQ + 3, o, S, tt(o, S), rope_cs[:, 1, :])
            dve.wait_ge(ps_free, 2 * (P_UQ + 4))
            for o in range(2):
                dve.tensor_tensor(AX[o], AX[o], tt(o, S), ALU.add).then_inc(s("qr_sum"), 1)
            for o in range(2):
                dve.wait_ge(s("q_hi"), 5 + o)
                dve.tensor_tensor(a_q(1, 4 + o), AX[o], a_q(0, 4 + o).bitcast(f32), ALU.subtract).then_inc(s("qr_lo"), 1)
            dve_lo(dve, 13, 1)
            for j in range(4):
                low(j, 6 + j + 1, P_UKV + j // 2, j % 2, a_k(1, j), a_k(0, j))
            for j in range(4):
                dve_take(dve, P_UKV + 2 + j // 2, j % 2, S, tt(2 + j, S))
            for g in range(4, 8):
                v_lo(g)
            dve_lo(dve, 14, 0)

            def mla_max(u):
                b, q = u % 4, u % 4
                n = P * (b + 1)
                dve.wait_ge(s("a_s"), u + 1)
                if u >= 4:
                    dve.wait_ge(s("a_tr"), u - 3)
                dve.tensor_tensor_reduce(out=tt(q, n), in0=ps[:, 4 * (u % 2), 0:n], in1=dist[:, S - n:S], scale=1.0,
                                         scalar=NEG, op0=ALU.add, op1=ALU.max, accum_out=cols[:, u:u + 1]).then_inc(s("a_max"), 1)
                dve.wait_ge(s("a_max"), u + 1)
                dve.tensor_scalar(cols[:, 16 + u:17 + u], cols[:, u:u + 1], -SC1, None, ALU.mult).then_inc(s("a_nmx"), 1)

            def mla_norm(u):
                n = P * (u % 4 + 1)
                dve.wait_ge(s("a_exp"), u + 1)
                once(dve, "a_rcp", u + 1, dve.reciprocal(cols[:, 48 + u:49 + u], cols[:, 32 + u:33 + u]))
                dve.tensor_scalar(tt(u % 4, n), tt(u % 4, n), cols[:, 48 + u:49 + u], None, ALU.mult).then_inc(s("a_norm"), 1)

            def mla_lo(u):
                n = P * (u % 4 + 1)
                dve.wait_ge(s("a_hi"), u + 1)
                dve.tensor_tensor(a_pt(1, u % 2, n), ps[:, 2 + 4 * (u % 2), 0:n], a_pt(0, u % 2, n).bitcast(f32),
                                  ALU.subtract).then_inc(s("a_lo"), 1)

            def mla_out(u):
                dve.wait_ge(s("a_zhi"), u + 1)
                hh, b = divmod(u, 4)
                dve.tensor_tensor(z_lo[:, hh, P * b:P * b + P], ps[:, 1 + 4 * (u % 2), P:2 * P],
                                  z_hi[:, hh, P * b:P * b + P].bitcast(f32), ALU.subtract).then_inc(s("a_zlo"), 1)
            mla_max(0)
            for u in range(18):
                if u + 1 < 16:
                    mla_max(u + 1)
                if 1 <= u < 17:
                    mla_lo(u - 1)
                if u < 16:
                    mla_norm(u)
                if u >= 2:
                    mla_out(u - 2)

            def out_tiles(b0, p0, ntok):
                for j in range(4):
                    if j or b0 != B_OUT1:
                        dve_lo(dve, b0 + j + 1, (b0 + j + 1) % 2)
                    for o in range(2):
                        dve_take(dve, p0 + j, o, ntok, ac(2 * j + o)[:, T - ntok:T])
            out_tiles(B_OUT1, P_OUT1, S)
            dve_post(dve, 0, S, META, nxt_c0=META)

            def add_acc(p, o, k, ntok):
                dve.wait_ge(ps_full, 2 * p + o + 1)
                dve.wait_ge(ps_free, 2 * p + o)
                dst = like(ac(k)[:, T - ntok:T], ntok)
                dve.tensor_tensor(dst, dst, banks(slot_of(p), o, ntok), ALU.add).then_inc(ps_free, 1)

            def slot_of(p):
                return p % 2
            done = 0
            R1 = rr[:, 0, META:T]
            for c, nt in enumerate(CHUNKS1):
                b0, p0 = B_MLP1 + done + 4 * c, P_MLP1 + done + 4 * c
                for j in range(nt):
                    dve_lo(dve, b0 + j + 1, (b0 + j + 1) % 2)
                    n = done + j
                    if n == 0:
                        dve_rstd(dve, 2, S, META)
                        dve.wait_ge(rstd, 3)
                    q = n % 2
                    dve_take(dve, p0 + j, 0, S, tt(q, S), R1)
                    dve_take(dve, p0 + j, 1, S, tt(4 + q, S), R1)
                    dve.wait_ge(s("sw_silu"), n + 1)
                    dve.wait_ge(ps_free, 2 * (p0 + j) + 2)
                    once(dve, "sw_hm", n + 1, dve.tensor_tensor(tt(4 + q, S), tt(4 + q, S), tt(2 + q, S), ALU.mult))
                    dve.wait_ge(s("sw_hi"), n + 1)
                    dve.tensor_tensor(a_hid(1, j)[:, 0:S], tt(4 + q, S), a_hid(0, j)[:, 0:S].bitcast(f32),
                                      ALU.subtract).then_inc(s("sw_lo"), 1)
                if c == 0:
                    dve.wait_ge(acc_zero, 1)
                for j in range(4):
                    if c == len(CHUNKS1) - 1 and j == 3:
                        for k in range(2):
                            dve.wait_ge(s("p_hi"), k + 1)
                            dve.tensor_tensor(a_ple(1, k), rope_cs[:, k, :], a_ple(0, k).bitcast(f32),
                                              ALU.subtract).then_inc(s("p_lo"), 1)
                    dve_lo(dve, b0 + nt + j + 1, (b0 + nt + j + 1) % 2)
                    for o in range(2):
                        add_acc(p0 + nt + j, o, 2 * j + o, S)
                done += nt
            def ple_proj(k):
                return (rope_cs[:, 0, :], rope_cs[:, 1, :], tt(0, S), tt(1, S), tt(4, S), tt(5, S), ac(0, S), ac(1, S))[k]

            def ple_take(k):
                dve_take(dve, P_PLEP + k // 2, k % 2, S, ple_proj(k))

            def ple_rest():
                dve.wait_ge(resid, 8 + 2)
                for k in range(4, KD):
                    ple_take(k)
            for k in range(4):
                ple_take(k)
            dve_lo(dve, B_PLEG, B_PLEG % 2)
            dve_post(dve, 1, S, META, nxt_c0=META, between=ple_rest)
            for k in range(KD):
                if k % 2 == 0:
                    dve_lo(dve, B_PLEG + k // 2 + 1, (B_PLEG + k // 2 + 1) % 2)
                dve.wait_ge(s("ple_s"), k + 1)
                a = ple_proj(k)
                dve.tensor_tensor(a, a, tt(2 + k % 2, S), ALU.mult).then_inc(ps_free, 1)
                dve.wait_ge(ps_free, 2 * P_PLEG + k + 1)
                dve.tensor_tensor(h[:, k, META:T], h[:, k, META:T], a, ALU.add).then_inc(s("ple_h"), 1)
            for k in range(KD):
                dve_zlo(dve, 3, k, 0)

            nb = 0

            def d_max(u):
                nonlocal nb
                head, b = divmod(u, 5)
                if b == 0:
                    slope = 2.0 ** (-8.0 * (head + 1) / DIFF_HEADS)
                    dve.tensor_scalar(ssum[:, :], dist[:, :], slope / SC2, None, ALU.mult).then_inc(s("d_bias"), 1)
                    dve.wait_ge(s("d_bias"), head + 1)
                off = S - P + META if b == 0 else S - P * b
                for c in range(2):
                    nq, nk, t = unit(u, c)
                    w = u % UG % 3 * 2 + c
                    dve.wait_ge(s("d_s"), 2 * u + c + 1)
                    if u % UG >= 3 and c == 0:
                        dve.wait_ge(s("d_tr"), u - 2)
                    sc = s_cut(u, c)
                    dve.tensor_tensor_reduce(out=like(t, nk), in0=sc, in1=like(ssum[0:nq, off:off + nk], nk), scale=1.0, scalar=NEG, op0=ALU.add, op1=ALU.max,
                                             accum_out=cols[0:nq, D_MAX + w:D_MAX + w + 1]).then_inc(s("d_max"), 1)
                    dve.wait_ge(s("d_max"), 2 * u + c + 1)
                    dve.tensor_scalar(cols[0:nq, D_NMX + w:D_NMX + w + 1], cols[0:nq, D_MAX + w:D_MAX + w + 1], -SC2, None,
                                      ALU.mult).then_inc(s("d_nmx"), 1)

            def d_mix(u):
                nq, nk, t0 = unit(u, 0)
                t1 = unit(u, 1)[2]
                w = u % UG % 3 * 2
                r0, r1 = (cols[0:nq, D_RC + w + c:D_RC + w + c + 1] for c in range(2))
                dve.wait_ge(s("d_exp"), 2 * u + 2)
                once(dve, "d_rc", 2 * u + 1, dve.reciprocal(cols[0:nq, D_RC + w:D_RC + w + 2], cols[0:nq, D_SUM + w:D_SUM + w + 2]))
                once(dve, "d_rc", 2 * u + 2, dve.tensor_tensor(r1, r1, cols[0:nq, 84:85], ALU.mult))
                once(dve, "d_m1", u + 1, dve.tensor_scalar(t1, t1, r1, None, ALU.mult))
                dve.scalar_tensor_tensor(t0, t0, r0, t1, op0=ALU.mult, op1=ALU.add).then_inc(s("d_a"), 1)

            def d_lo(u):
                nq, nk, _ = unit(u, 0)
                dve.wait_ge(s("d_hi"), d_parts(u))
                dve.tensor_tensor(a_dpt(1, u % 2, 0, META)[:, 0:nq], ps[0:META, t_bank(u) + 2 + u % 2, 0:nq],
                                  a_dpt(0, u % 2, 0, META)[:, 0:nq].bitcast(f32), ALU.subtract).then_inc(s("d_lo"), 1)
                if nk > META:
                    nt = (nk - META) // P
                    dve.tensor_tensor(a_dpt(1, u % 2, 1, P, nt), ps[:, t_bank(u) + u % 2, 0:nk - META],
                                      a_dpt(0, u % 2, 1, P, nt).bitcast(f32), ALU.subtract).then_inc(s("d_lo"), 1)

            def d_out(u):
                head, b = divmod(u, 5)
                nq = unit(u, 0)[0]
                q0 = 0 if b == 0 else META + P * (b - 1)
                dve.wait_ge(s("d_pv"), u + 1)
                dve.tensor_copy(ac(head)[:, q0:q0 + nq], ps[:, t_bank(u) + 2 + u % 2, 2 * P:2 * P + nq]).then_inc(s("d_o"), 1)

            def sub_scale(g):
                for i in range(2):
                    dve.wait_ge(s("d_root"), 2 * g + i + 1)
                    dve.reciprocal(sq[:, i, :], sq[:, i, :]).then_inc(s("d_n"), 1)
                for i in range(2):
                    k = 2 * g + i
                    dve.wait_ge(s("d_n"), 4 * g + i + 1)
                    dve.scalar_tensor_tensor(ac(k), ac(k), smc("subln"), sq[:, i, :], op0=ALU.mult, op1=ALU.mult).then_inc(s("d_n"), 1)
                for i in range(2):
                    k = 2 * g + i
                    dve.wait_ge(s("d_ohi"), k + 1)
                    dve.tensor_tensor(a_out(1, k), ac(k), a_out(0, k).bitcast(f32), ALU.subtract).then_inc(s("d_olo"), 1)

            for g in range(GROUPS):
                b0, p0 = B_QKV + 3 * g, P_QKV + 3 * g
                for i in range(2):
                    dve_lo(dve, b0 + i + 1, (b0 + i + 1) % 2)
                    if g == 0 and i == 0:
                        dve_rstd(dve, 4, T, 0)
                        dve.wait_ge(rstd, 5)
                    for o in range(2):
                        dve_take(dve, p0 + i, o, T, tt(2 * i + o), rr[:, 0, :])
                    if g and i == 0:
                        d_out(UG * g - 1)
                    for o in range(2):
                        dve.wait_ge(s("dq_hi"), 4 * g + 2 * i + o + 1)
                        dve.tensor_tensor(a_qk(1, o, i), tt(2 * i + o), a_qk(0, o, i).bitcast(f32),
                                          ALU.subtract).then_inc(s("dq_lo"), 1)
                    if g and i == 0:
                        sub_scale(g - 1)
                dve_lo(dve, b0 + 3, (b0 + 3) % 2)
                for i in range(2):
                    dve_take(dve, p0 + 2, i, T, tt(4 + i), rr[:, 0, :])
                if g == 0:
                    dve.wait_ge(s("dist"), 2)
                first = UG * g
                tb = t_bank(first)
                d_max(first)
                for i in range(2):
                    dve.wait_ge(s("dv_hi"), 4 * g + 2 * i + 2)
                    dve.tensor_tensor(a_dv(1, i, 1, P, 4), ps[:, tb + i, :], a_dv(0, i, 1, P, 4).bitcast(f32),
                                      ALU.subtract).then_inc(s("dv_lo"), 1)
                    dve.tensor_tensor(a_dv(1, i, 0, META), ps[0:META, tb + 2 + i, 0:P], a_dv(0, i, 0, META).bitcast(f32),
                                      ALU.subtract).then_inc(s("dv_lo"), 1)
                for u in range(first, first + UG + 1):
                    if u + 1 < first + UG:
                        d_max(u + 1)
                    if u >= first + 2:
                        d_out(u - 2)
                    if first < u <= first + UG:
                        d_lo(u - 1)
                    if u < first + UG:
                        d_mix(u)
            d_out(UG * GROUPS - 1)
            sub_scale(GROUPS - 1)
            out_tiles(B_OUT2, P_OUT2, T)
            dve_post(dve, 2, T, 0, nxt_c0=0)

            def dve_mlp(l, b0, p0, si, ntok):
                r = rr[:, 0, T - ntok:T]

                def chunk(c, last=False):
                    head = isinstance(c, int) and c == 0
                    for j in range(KD // 2):
                        dve_lo(dve, b0 + j + 1 + 8 * c, (b0 + j + 1) % 2)
                        if head and j == 0:
                            dve_rstd(dve, si, ntok, T - ntok)
                            dve.wait_ge(rstd, si + 1)
                        for o in range(2):
                            n = 2 * (p0 + j) + o + 1 + 16 * c
                            dve.wait_ge(ps_full, n)
                            dve.scalar_tensor_tensor(like(tt(o, ntok), ntok), banks((p0 + j) % 2, o, ntok), 0.0,
                                                     like(r, ntok), op0=ALU.max, op1=ALU.mult).then_inc(ps_free, 1)
                        for o in range(2):
                            n = FF2 * l + 2 * j + o + 8 * c
                            dve.wait_ge(s("hid_hi"), n + 1)
                            dve.tensor_tensor(a_hid(1, 2 * j + o)[:, 0:ntok], tt(2 + o, ntok),
                                              a_hid(0, 2 * j + o)[:, 0:ntok].bitcast(f32), ALU.subtract).then_inc(s("hid_lo"), 1)
                    if head:
                        dve.wait_ge(acc_zero, 2 + l)
                    for j in range(4, 8):
                        if not (last and j == 7):
                            dve_lo(dve, b0 + j + 1 + 8 * c, (b0 + j + 1) % 2)
                        for o in range(2):
                            n = 2 * (p0 + j) + o + 16 * c
                            dve.wait_ge(ps_full, n + 1)
                            dve.wait_ge(ps_free, n)
                            dst = like(ac(2 * (j - 4) + o)[:, T - ntok:T], ntok)
                            dve.tensor_tensor(dst, dst, banks((p0 + j) % 2, o, ntok), ALU.add).then_inc(ps_free, 1)
                return chunk
            mlp = dve_mlp(0, B_MLP2, P_MLP2, 6, T)
            mlp(0)
            with dve.Fori(1, NCH2) as c:
                mlp(c)
            dve_post(dve, 3, T, 0, nxt_c0=0)
            for m in range(4):
                b0, p0 = B_CONV + 3 * m, P_CONV + 3 * m
                for i in range(2):
                    dve_lo(dve, b0 + i + 1, (b0 + i + 1) % 2)
                    if m == 0 and i == 0:
                        dve_rstd(dve, 8, T, 0)
                        dve.wait_ge(rstd, 9)
                    j = 2 * m + i
                    if j >= 2:
                        dve.wait_ge(s("sc_lo"), 2 * m)
                    dve_take(dve, p0 + i, 0, T, tt(0), rr[:, 0, :])
                    dve_take(dve, p0 + i, 1, T, tt(1), rr[:, 0, :])
                    dve.wait_ge(ps_free, 2 * (p0 + i) + 2)
                    once(dve, "sc_v", j + 1, dve.tensor_tensor(tt(2 + i), tt(0), tt(1), ALU.mult))
                    dve.wait_ge(s("sc_y"), j + 1)
                    for t in range(2):
                        once(dve, "sc_acc", 2 * j + t + 1, dve.scalar_tensor_tensor(
                            tt(4 + i, S), tt(2 + i)[:, META - 2 + t:T - 2 + t], smc("conv2_w", 8 * t + j), tt(4 + i, S),
                            op0=ALU.mult, op1=ALU.add))
                dve_lo(dve, b0 + 3, (b0 + 3) % 2)
                for i in range(2):
                    j = 2 * m + i
                    dve.wait_ge(ps_full, 2 * (p0 + 2) + i + 1)
                    b = 4 * ((p0 + 2) % 2) + 2 * i
                    dve.tensor_tensor(like(tt(i), T), banks((p0 + 2) % 2, i, T), like(rr[:, 0, :], T), ALU.mult).then_inc(ps_free, 1)
                    dve.wait_ge(ps_free, 2 * (p0 + 2) + i + 1)
                    once(dve, "sc_o", j + 1, dve.tensor_tensor(tt(i, S), tt(i)[:, META:T], tt(4 + i, S), ALU.mult))
                for i in range(2):
                    j = 2 * m + i
                    dve.wait_ge(s("sc_hi"), j + 1)
                    dve.tensor_tensor(a_out(1, j, 0, S), tt(i, S), a_out(0, j, 0, S).bitcast(f32), ALU.subtract).then_inc(s("sc_lo"), 1)
            out_tiles(B_OUT3, P_OUT3, S)
            dve_post(dve, 4, S, META, nxt_c0=META)
            mlp = dve_mlp(1, B_MLP3, P_MLP3, 10, S)
            mlp(0)
            with dve.Fori(1, NCH2 - 1) as c:
                mlp(c)
            mlp(NCH2 - 1, last=True)
            dve_post(dve, 5, S, META)

        @block.tensor
        def _(pe):
            def three(dst, lh, rh, start, stop):
                pe.matmul(dst, lh(0), rh(0), start=start, stop=False)
                pe.matmul(dst, lh(0), rh(1), start=False, stop=False)
                return pe.matmul(dst, lh(1), rh(0), start=False, stop=stop)

            def gemm(b, ntok=S, z=z_part, nk=KD, z_ready=None, sub=0, p=None):
                p = pair_of(b) + sub if p is None else p
                pe.wait_ge(wlo, b + 1)
                project(pe, b % 2, p % 2, 2 * sub, nk, z, ntok, 2 * (p - 1) if p >= 2 else None, z_ready)

            def stat_after(b, si, ntok, c0):
                pe_stat(pe, si, (pair_of(b) + 1) % 2, ntok, c0)
                pe.wait_ge(rooted, si + 1)
            pe.wait_ge(consts, 16)
            gemm(0, z_ready=z_ready_for(pe, 0))
            stat_after(0, 0, S, META)
            gemm(1)
            gemm(2)
            pe.wait_ge(s("c_sq"), 3)
            pe_columns(pe, ps[:, 1, :], [c_square(0), c_square(1)], S).then_inc(s("c_stat"), 1)
            pe_columns(pe, ps[:, 5, :], [c_square(2)], S).then_inc(s("c_stat"), 1)
            gemm(3)
            pe.wait_ge(s("c_rcp"), 1)
            pe_spread(pe, 3, cols[:, R_COL:R_COL + 4], S).then_inc(s("c_spread"), 1)
            pe_spread(pe, 7, cols[:, R_COL + 4:R_COL + 8], S).then_inc(s("c_spread"), 1)
            for b in range(4, 9):
                gemm(b)

            def v_transpose(g, src):
                if g >= 2:
                    pe.wait_ge(s("v_lo"), g - 1)
                for t in range(4):
                    last = pe.transpose(ps[:, 3 + 4 * (g % 2), t * P:t * P + P], src[:, t * P:t * P + P], ident[:, :])
                last.then_inc(s("v_tr"), 1)
            pe.wait_ge(s("c_norm"), 3)
            pe.wait_ge(ps_free, 2 * 8)
            v_transpose(0, tt(0, S))
            v_transpose(1, tt(1, S))
            gemm(9)
            pe.wait_ge(ps_free, 2 * 9)
            v_transpose(2, tt(2, S))
            v_transpose(3, tt(3, S))
            gemm(10)
            pe.wait_ge(s("g"), 11)
            for t in range(4):
                last = pe.transpose(ps[:, 1, 4 * t:4 * t + 4], G0[0:4, t * P:t * P + P], ident[0:4, 0:4])
            last.then_inc(s("g_tr"), 1)
            pe.wait_ge(s("sel"), 2)
            pe.wait_ge(ps_free, 2 * 11)
            pe.wait_ge(s("cv_lo"), 8)
            pe.wait_ge(s("v_lo"), 4)
            pe.wait_ge(s("gc"), 1)

            def m_bc(hh):
                sel = ssum[0:4, hh * P:hh * P + P]
                if hh:
                    pe.wait_ge(s("m_e"), 8 * hh)
                pe.matmul(ps[:, 1, :], sel, AX[0][0:4, :], start=True, stop=True)
                pe.matmul(ps[:, 5, :], sel, AX[1][0:4, :], start=True, stop=True).then_inc(s("bc"), 1)

            def m_scores(hh):
                if hh:
                    pe.wait_ge(s("m_p"), 4 * hh)
                for kb in range(4):
                    b, at = [(0, 0), (2, 0), (4, 0), (2, KB_N[1])][kb]
                    last = three(ps[:, b, at:at + KB_N[kb]], lambda x: a_mqk(x, 4 + hh)[:, kb * P:kb * P + P],
                                 lambda x: a_mqk(x, hh)[:, kb * P:S], True, True)
                last.then_inc(s("m_s"), 1)
            m_bc(0)
            m_scores(0)
            for hh in range(4):
                if hh < 3:
                    m_bc(hh + 1)
                    m_scores(hh + 1)
                pe.wait_ge(s("m_lo"), hh + 1)
                if hh:
                    pe.wait_ge(s("m_h"), 6 * hh)
                for kb in range(4):
                    three(ps[:, 6, kb * P:S], lambda x: a_v(x, hh)[:, kb * P:kb * P + P],
                          lambda x: a_p(x, KB_AT[kb], KB_N[kb]), kb == 0, kb == 3)
                for kb in range(4):
                    pe.matmul(ps[:, 7, kb * P:S], ones_r[:, :], a_p(0, KB_AT[kb], KB_N[kb]), start=(kb == 0), stop=False)
                    last = pe.matmul(ps[:, 7, kb * P:S], ones_r[:, :], a_p(1, KB_AT[kb], KB_N[kb]), start=False, stop=(kb == 3))
                last.then_inc(s("m_nd"), 1)
                pe.wait_ge(s("m_sq"), hh + 1)
                pe.matmul(ps[:, 3, :], ones[:, :], rr[:, 1, 0:S], start=True, stop=True).then_inc(s("m_st"), 1)

            def c_part(x, k):
                return a_c(x, k)

            def ckv_part(x, k):
                return a_c(x, 2)
            pe.wait_ge(s("m_h"), 24)
            for sub in range(4):
                gemm(B_UQ, z=c_part, nk=2, sub=sub)
            for sub in range(4):
                gemm(B_UKV, z=ckv_part, nk=1, sub=sub)
            for g in range(4, 8):
                pe.wait_ge(ps_free, 2 * (P_UKV + 2) + g - 4 + 1)
                pe.wait_ge(s("v_lo"), g - 1)
                if g == 4:
                    pe.wait_ge(s("m_root"), 4)
                for t in range(4):
                    last = pe.transpose(ps[:, 3 + 4 * (g % 2), t * P:t * P + P], tt(2 + g - 4, S)[:, t * P:t * P + P], ident[:, :])
                last.then_inc(s("v_tr"), 1)
            pe.wait_ge(s("v_lo"), 8)
            pe.wait_ge(s("qr_lo"), 2)
            pe.wait_ge(ps_free, 2 * (P_UKV + 4))

            def mla_s(u):
                hh, b = divmod(u, 4)
                n = P * (b + 1)
                if u >= 2:
                    pe.wait_ge(s("a_max"), u - 1)
                n = max(n, 2 * P)
                dst = ps[:, 4 * (u % 2), 0:n]
                three(dst, lambda x: a_q(x, hh)[:, b * P:b * P + P], lambda x: a_k(x, hh)[:, 0:n], True, False)
                three(dst, lambda x: a_q(x, 4 + hh // 2)[:, b * P:b * P + P], lambda x: a_kpe(x, hh % 2)[:, 0:n],
                      False, True).then_inc(s("a_s"), 1)

            def mla_t(u):
                pe.wait_ge(s("a_norm"), u + 1)
                if u >= 2:
                    pe.wait_ge(s("a_lo"), u - 1)
                for kb in range(u % 4 + 1):
                    last = pe.transpose(ps[:, 2 + 4 * (u % 2), kb * P:kb * P + P], tt(u % 4)[:, kb * P:kb * P + P], ident[:, :])
                last.then_inc(s("a_tr"), 1)

            def mla_pv(u):
                hh = u // 4
                pe.wait_ge(s("a_lo"), u + 1)
                if u >= 2:
                    pe.wait_ge(s("a_zlo"), u - 1)
                for kb in range(u % 4 + 1):
                    last = three(ps[:, 1 + 4 * (u % 2), 0:2 * P], lambda x: a_v(x, hh)[:, kb * P:kb * P + P],
                                 lambda x: a_pt(x, u % 2, 2 * P, (kb - 1) * P), kb == 0, kb == u % 4)
                last.then_inc(s("a_pv"), 1)
            mla_s(0)
            mla_s(1)
            for u in range(17):
                if u + 2 < 16:
                    mla_s(u + 2)
                if u >= 1:
                    mla_pv(u - 1)
                if u < 16:
                    mla_t(u)
            pe.wait_ge(s("a_zlo"), 16)
            pe.wait_ge(s("m_zlo"), 4)
            for j in range(4):
                gemm(B_OUT1 + j)
            pe_post_stat(pe, 0, S, META)

            def hid_part(x, k):
                return a_hid(x, k)
            done = 0
            for c, nt in enumerate(CHUNKS1):
                b0 = B_MLP1 + done + 4 * c
                for j in range(nt):
                    first = done + j == 0
                    gemm(b0 + j, z_ready=z_ready_for(pe, 1) if first else None)
                    if first:
                        stat_after(b0, 2, S, META)
                for j in range(4):
                    gemm(b0 + nt + j, z=hid_part, nk=nt, z_ready=(lambda k: pe.wait_ge(s("sw_lo"), done + k + 1)) if j == 0 else None)
                done += nt
            pe.wait_ge(s("p_lo"), 2)
            for sub in range(4):
                gemm(B_PLEP, z=lambda x, k: a_ple(x, k), nk=2, sub=sub)
                if sub == 1:
                    pe_post_stat(pe, 1, S, META)
            for j in range(4):
                gemm(B_PLEG + j, z_ready=z_ready_for(pe, 2) if j == 0 else None)

            def d_s(u):
                i, b = (u // 5) % 2, u % 5
                nq, nk, _ = unit(u, 0)
                q0 = 0 if b == 0 else META + P * (b - 1)
                for c in range(2):
                    r = slice(64 * c, 64 * c + 64)
                    back = 1 if b in (0, 4) else 2
                    if u % UG >= back:
                        pe.wait_ge(s("d_max"), 2 * (u - back) + c + 1)
                    sb0 = s_bank(u) + 2 * c + (b % 2)
                    for cut, (a, e) in enumerate([(0, max(nk, 2 * P) if b else nk)] if nk <= 512 else [(0, HALF), (HALF, T)]):
                        last = three(ps[:, sb0 + cut, 0:e - a], lambda x: a_qk(x, 0, i)[r, q0:q0 + P],
                                     lambda x: a_qk(x, 1, i)[r, a:e], True, True)
                    last.then_inc(s("d_s"), 1)

            def d_t(u):
                nq, nk, t = unit(u, 0)
                pe.wait_ge(s("d_a"), u + 1)
                if u % UG >= 2:
                    pe.wait_ge(s("d_lo"), d_parts(u - 2))
                    pe.wait_ge(s("d_o"), u - 1)
                last = pe.transpose(ps[0:META, t_bank(u) + 2 + u % 2, 0:nq], t[:, 0:META], ident[0:nq, 0:nq])
                for kb in range((nk - META) // P):
                    last = pe.transpose(ps[:, t_bank(u) + u % 2, kb * P:kb * P + P], t[:, META + kb * P:META + kb * P + P], ident[:, :])
                last.then_inc(s("d_tr"), 1)

            def d_pv(u):
                i = (u // 5) % 2
                nq, nk, _ = unit(u, 0)
                pe.wait_ge(s("d_lo"), d_parts(u))
                nt = (nk - META) // P
                a = 0 if nt else P
                dst = ps[:, t_bank(u) + 2 + u % 2, P + a:2 * P + nq]
                last = three(dst, lambda x: a_dv(x, i, 0, META), lambda x: a_dpt(x, u % 2, -1, META, 2)[:, a:P + nq], True, nt == 0)
                for t in range(1, nt + 1):
                    last = three(dst, lambda x: a_dv(x, i, t), lambda x: a_dpt(x, u % 2, t - 1, P, 2), False, t == nt)
                last.then_inc(s("d_pv"), 1)

            def sub_stat(g, base):
                for i in range(2):
                    pe.wait_ge(s("d_sq"), 2 * g + i + 1)
                    for c in range(2):
                        last = pe.matmul(ps[:, base + 2 * i + c, 0:HALF], ones[:, :], sq[:, i, c * HALF:(c + 1) * HALF],
                                         start=True, stop=True)
                    last.then_inc(s("d_st"), 1)

            gemm(B_QKV, T, z_ready=z_ready_for(pe, 3))
            stat_after(B_QKV, 4, T, 0)
            for g in range(GROUPS):
                b0, p0 = B_QKV + 3 * g, P_QKV + 3 * g
                if g:
                    sub_stat(g - 1, 4 * ((p0 + 1) % 2))
                    pe.wait_ge(s("d_root"), 2 * g)
                gemm(b0 + 1, T)
                gemm(b0 + 2, T)
                first = UG * g
                pe.wait_ge(s("dq_lo"), 4 * g + 4)
                d_s(first)
                pe.wait_ge(ps_free, 2 * (p0 + 3))
                tb = t_bank(first)
                for i in range(2):
                    for t in range(4):
                        pe.transpose(ps[:, tb + i, t * P:t * P + P], tt(4 + i)[:, META + t * P:META + t * P + P], ident[:, :])
                    pe.transpose(ps[0:META, tb + 2 + i, 0:P], tt(4 + i)[:, 0:META], ident[:, :]).then_inc(s("dv_tr"), 1)
                d_s(first + 1)
                pe.wait_ge(s("dv_lo"), 4 * g + 4)
                for u in range(first, first + UG):
                    if u + 2 < first + UG:
                        d_s(u + 2)
                    if u > first:
                        d_pv(u - 1)
                    d_t(u)
                if g + 1 < GROUPS:
                    pe.wait_ge(s("d_max"), 2 * UG * (g + 1))
                    gemm(b0 + 3, T)
                d_pv(first + UG - 1)
            sub_stat(GROUPS - 1, 0)

            def out_part(x, k):
                return a_out(x, k)
            pe.wait_ge(s("d_olo"), 8)
            pe.wait_ge(s("d_o"), UG * GROUPS)
            for j in range(4):
                gemm(B_OUT2 + j, T, z=out_part)
            pe_post_stat(pe, 2, T, 0)

            def pe_mlp(l, b0, p0, zi, si, ntok):
                def chunk(c):
                    head = isinstance(c, int) and c == 0
                    for j in range(8):
                        pe.wait_ge(wlo, b0 + j + 1 + 8 * c)
                        if head and j == 1:
                            pe.wait_ge(rooted, si + 1)
                        if j < 4:
                            ready = z_ready_for(pe, zi) if head and j == 0 else None
                        else:
                            ready = (lambda k: pe.wait_ge(s("hid_lo"), FF2 * l + k + 1 + 8 * c)) if j == 4 else None
                        project(pe, (b0 + j) % 2, (p0 + j) % 2, 0, KD, z_part if j < 4 else hid_part, ntok,
                                2 * (p0 + j - 1) + 16 * c, ready)
                        if head and j == 0:
                            pe_stat(pe, si, (p0 + 1) % 2, ntok, T - ntok)
                return chunk
            mlp = pe_mlp(0, B_MLP2, P_MLP2, 4, 6, T)
            mlp(0)
            with pe.Fori(1, NCH2) as c:
                mlp(c)
            pe_post_stat(pe, 3, T, 0)
            for j in range(12):
                gemm(B_CONV + j, T, z_ready=z_ready_for(pe, 5) if j == 0 else None)
                if j == 0:
                    stat_after(B_CONV, 8, T, 0)
            for j in range(4):
                gemm(B_OUT3 + j, S, z=out_part, z_ready=(lambda k: pe.wait_ge(s("sc_lo"), k + 1)) if j == 0 else None)
            pe_post_stat(pe, 4, S, META)
            mlp = pe_mlp(1, B_MLP3, P_MLP3, 6, 10, S)
            mlp(0)
            with pe.Fori(1, NCH2) as c:
                mlp(c)
            pe_post_stat(pe, 5, S, META)


def pack_weights(w_in, w_uq, w_ukv, w_out, w_gate, w_up, w_down, w_ple_proj, w_ple_gate, w_in_2, w_out_2, w_up_2, w_down_2):
    stream = np.zeros((NBLK, P, BLK), np.float32)
    n = 0

    def block(*tiles):
        nonlocal n
        at = 0
        for t in tiles:
            k = t.shape[0] // P
            stream[n, :, at:at + k * P] = t.reshape(k, P, P).transpose(1, 0, 2).reshape(P, k * P)
            at += k * P
        n += 1

    def col(w, c):
        return w[:, c:c + P]
    CKV, KR, MQ, MK, MV, MO, MI, MF = 256, 384, 448, 960, 1472, 1984, 2496, 2500
    block(col(w_in, 0), col(w_in, P))
    gates = np.zeros((D, P), np.float32)
    gates[:, 0:4], gates[:, 32:36] = w_in[:, MI:MI + 4], w_in[:, MF:MF + 4]
    block(col(w_in, CKV), gates)
    t1, t2 = w_in[:, KR:KR + 32], w_in[:, KR + 32:KR + 64]
    block(np.concatenate([t1, t2, t1, t2], 1), np.concatenate([t2, t1, t2, t1], 1))
    for base in (MQ, MK, MV, MO):
        for j in range(0, 4, 2):
            block(col(w_in, base + j * P), col(w_in, base + (j + 1) * P))
    q = [w_uq[:, QKD * i:QKD * (i + 1)] for i in range(4)]
    pe = [x[:, 128:192] for x in q]
    swap = [np.concatenate([x[:, 32:64], x[:, 0:32]], 1) for x in pe]
    block(*[x[:, 0:P] for x in q], np.concatenate(pe[0:2], 1), np.concatenate(pe[2:4], 1),
          np.concatenate(swap[0:2], 1), np.concatenate(swap[2:4], 1))
    block(*[col(w_ukv, 256 * i) for i in range(4)], *[col(w_ukv, 256 * i + P) for i in range(4)])

    def columns(w):
        for j in range(0, w.shape[1] // P, 2):
            block(col(w, j * P), col(w, (j + 1) * P))
    columns(w_out)
    done = 0
    for nt in CHUNKS1:
        for j in range(done, done + nt):
            block(col(w_gate, j * P), col(w_up, j * P))
        columns(w_down[done * P:(done + nt) * P])
        done += nt
    block(*[col(w_ple_proj, j * P) for j in range(KD)])
    columns(w_ple_gate)
    for g in range(GROUPS):
        for i in range(2):
            block(col(w_in_2[0], (2 * g + i) * P), col(w_in_2[0], D + (2 * g + i) * P))
        block(col(w_in_2[0], 2 * D + 2 * g * P), col(w_in_2[0], 2 * D + (2 * g + 1) * P))
    columns(w_out_2[0])

    def mlp(up, down):
        for c in range(NCH2):
            columns(up[:, c * D:(c + 1) * D])
            columns(down[c * D:(c + 1) * D])
    mlp(w_up_2[0], w_down_2[0])
    for m in range(4):
        for i in range(2):
            block(col(w_in_2[1], D + (2 * m + i) * P), col(w_in_2[1], 2 * D + (2 * m + i) * P))
        block(col(w_in_2[1], 2 * m * P), col(w_in_2[1], (2 * m + 1) * P))
    columns(w_out_2[1])
    mlp(w_up_2[1], w_down_2[1])
    assert n == NBLK
    return stream


def tiles(v):
    v = np.asarray(v, np.float32)
    v = v.reshape(-1, v.shape[-1] // P, P)
    return v.transpose(2, 0, 1).reshape(P, -1)


def pack_small(i):
    small = np.zeros((P, NSMALL), np.float32)

    def put(name, a):
        small[0:a.shape[0], SMALL[name]:SMALL[name] + a.shape[1]] = a
    for name, key in [("attn_pre", "attn_pre_norm"), ("attn_post", "attn_post_norm"), ("ffn_pre", "ffn_pre_norm"),
                      ("ffn_post", "ffn_post_norm"), ("q_norm", "q_norm"), ("kv_norm", "kv_norm"), ("conv_b", "conv_b"),
                      ("mlstm_norm", "mlstm_norm"), ("norm2", "norm_g_2"), ("conv_w", "conv_w"), ("conv2_w", "conv_w_2"),
                      ("subln", "subln_g_2")]:
        put(name, tiles(i[key]))
    put("gate_i", np.asarray(i["gate_bias_i"]).reshape(4, 1))
    put("gate_f", np.asarray(i["gate_bias_f"]).reshape(4, 1))
    f = (np.float32(10000.0) ** (-np.arange(0, 64, 2, dtype=np.float32) / np.float32(64))).astype(np.float32)
    put("freq", np.tile(f, 4).reshape(P, 1))
    put("sfreq", np.tile(np.concatenate([-f, f]), 2).reshape(P, 1))
    return small


def host_arrays(i):
    i = {k: np.asarray(v) for k, v in i.items()}
    return {
        "wstream": pack_weights(i["w_in"][0], i["w_uq"][0], i["w_ukv"][0], i["w_out"][0], i["w_gate"][0], i["w_up"][0],
                                i["w_down"][0], i["w_ple_proj"][0], i["w_ple_gate"][0], i["w_in_2"], i["w_out_2"],
                                i["w_up_2"], i["w_down_2"]),
        "xT": np.ascontiguousarray(i["x"].reshape(S, KD, P).transpose(1, 2, 0)),
        "metaT": np.ascontiguousarray(i["meta_tokens_2"].reshape(META, KD, P).transpose(2, 1, 0)),
        "pT": np.ascontiguousarray(i["p"].reshape(S, 2, P).transpose(2, 1, 0)).reshape(P, 2 * S),
        "pos": np.ascontiguousarray(np.broadcast_to(i["positions"].reshape(1, S), (P, S))),
        "small": pack_small(i),
        "lam": np.ascontiguousarray(np.broadcast_to(i["lambda_params_2"].reshape(1, 256), (P, 256))),
    }


def kernel(**inputs):
    import concourse.bacc as bacc
    from concourse.bass_utils import run_bass_kernel_spmd

    nc = bacc.Bacc("TRN2", target_bir_lowering=False, num_devices=1, dynamic_dma_scratch_size=256)
    arrays = host_arrays(inputs)
    args = {n: nc.dram_tensor(n, a.shape, mybir.dt.from_np(a.dtype), kind="ExternalInput").ap() for n, a in arrays.items()}
    out = nc.dram_tensor("out", (KD, P, S), mybir.dt.float32, kind="ExternalOutput").ap()
    build(nc, out=out, **args)
    r = run_bass_kernel_spmd(nc, [arrays], core_ids=[0])
    y = r.results[0]["out"]
    return np.ascontiguousarray(np.asarray(y).transpose(2, 0, 1).reshape(1, S, D))
```
